# Optimizing a Trainium2 kernel written in Bass

```python
import jax, jax.numpy as jnp
from jax import lax
import numpy as np

D_MODEL = 1024
BATCH = 1
SEQ = 128
DEPTH = 2
DEC_BATCH = 1
DEC_SEQ = 256
PAST_LEN = 128

GRID_W = 64
MIX_WIDTH = D_MODEL
MLA_HEADS = 8
QK_NOPE = 64
QK_ROPE = 32
QK_HEAD = QK_NOPE + QK_ROPE
V_HEAD = 64
Q_LORA = D_MODEL // 4
KV_LORA = D_MODEL // 8
MLA_WIDTH = MLA_HEADS * V_HEAD
CONV_CH = D_MODEL // 4
CONV_K = 31
NA_HEADS = 4
NA_HEAD_DIM = 64
NA_WIDTH = NA_HEADS * NA_HEAD_DIM
NA_WIN_H = 8
NA_WIN_W = 16
N_EXPERTS = 16
N_GROUPS = 4
EXPERTS_PER_GROUP = N_EXPERTS // N_GROUPS
TOP_K = 2
EXPERT_FF = D_MODEL // 2
ROPE_THETA = 10000.0
Q_BLOCK = 128
EPS = 1e-6
NEG_INF = -1e30
MLA_SCALE = QK_HEAD ** -0.5
NA_SCALE = NA_HEAD_DIM ** -0.5
OFF_Q = Q_LORA
OFF_KV = OFF_Q + KV_LORA
OFF_KR = OFF_KV + QK_ROPE
OFF_CONV = OFF_KR + 2 * CONV_CH
IN_COLS = OFF_CONV + 3 * NA_WIDTH
IN_SPLITS = (OFF_Q, OFF_KV, OFF_KR, OFF_CONV)

kernel_name = 'hybrid_mla_conformer_natten_moe_dit_step'

def rms_norm(x, g):
    xf = x.astype(jnp.float32)
    y = xf * lax.rsqrt(jnp.mean(xf * xf, axis=-1, keepdims=True) + EPS)
    return (y * g.astype(jnp.float32)).astype(x.dtype)

def layer_norm(x, g, b):
    xf = x.astype(jnp.float32)
    xc = xf - jnp.mean(xf, axis=-1, keepdims=True)
    var = jnp.mean(xc * xc, axis=-1, keepdims=True)
    return (xc * lax.rsqrt(var + EPS) * g.astype(jnp.float32) + b.astype(jnp.float32)).astype(x.dtype)

def modulation(cond, w_ada, b_ada):
    mod = jnp.dot(jax.nn.silu(cond), w_ada) + b_ada
    return jnp.split(mod, 6, axis=-1)

def axial_rope_tables(n_tokens):
    t = jnp.arange(n_tokens, dtype=jnp.int32)
    row = (t // GRID_W).astype(jnp.float32)
    col = (t % GRID_W).astype(jnp.float32)
    n_freq = QK_ROPE // 4
    inv_freq = ROPE_THETA ** (-jnp.arange(n_freq, dtype=jnp.float32) / n_freq)
    ang = jnp.concatenate([row[:, None] * inv_freq, col[:, None] * inv_freq], axis=-1)
    return jnp.cos(ang), jnp.sin(ang)

def rotate_tail(x, cos, sin):
    xr = x[..., QK_NOPE:].astype(jnp.float32)
    xp = xr.reshape(xr.shape[:-1] + (QK_ROPE // 2, 2))
    x1, x2 = xp[..., 0], xp[..., 1]
    cs = cos[:, None, :]
    sn = sin[:, None, :]
    rot = jnp.stack([x1 * cs - x2 * sn, x1 * sn + x2 * cs], axis=-1).reshape(xr.shape)
    return jnp.concatenate([x[..., :QK_NOPE], rot.astype(x.dtype)], axis=-1)

def blocked_attention(q, k, v, scale):
    bsz, n_q, n_h, d_q = q.shape
    qb = jnp.moveaxis(q.reshape(bsz, n_q // Q_BLOCK, Q_BLOCK, n_h, d_q), 1, 0)

    def one_block(qi):
        s = jnp.einsum('bqhd,bkhd->bhqk', qi, k).astype(jnp.float32) * scale
        p = jax.nn.softmax(s, axis=-1)
        return jnp.einsum('bhqk,bkhd->bqhd', p.astype(v.dtype), v)

    o = lax.map(one_block, qb)
    return jnp.moveaxis(o, 0, 1).reshape(bsz, n_q, n_h, v.shape[-1])

def mla_queries(q_lat, q_a_g, w_q_up, q_norm_g):
    q = jnp.dot(rms_norm(q_lat, q_a_g), w_q_up)
    q = q.reshape(q.shape[:2] + (MLA_HEADS, QK_HEAD))
    return rms_norm(q, q_norm_g)

def mla_keys_values(ckv_n, krope, w_kv_up, k_norm_g):
    kv = jnp.dot(ckv_n, w_kv_up).reshape(ckv_n.shape[:2] + (MLA_HEADS, QK_NOPE + V_HEAD))
    k_nope, v = kv[..., :QK_NOPE], kv[..., QK_NOPE:]
    k_rope = jnp.broadcast_to(krope[:, :, None, :], krope.shape[:2] + (MLA_HEADS, QK_ROPE))
    k = rms_norm(jnp.concatenate([k_nope, k_rope], axis=-1), k_norm_g)
    return k, v

def conformer_conv(u, dw_w, dw_b, ln_g, ln_b):
    a, g = jnp.split(u, 2, axis=-1)
    h = a * jax.nn.sigmoid(g)
    pad = CONV_K // 2
    h = lax.conv_general_dilated(h, dw_w[:, None, :].astype(h.dtype), window_strides=(1,),
                                 padding=[(pad, pad)], dimension_numbers=('NWC', 'WIO', 'NWC'),
                                 feature_group_count=CONV_CH) + dw_b
    return jax.nn.silu(layer_norm(h, ln_g, ln_b))

def na_heads(na_qkv, q_g, k_g):
    q, k, v = jnp.split(na_qkv, 3, axis=-1)
    shp = na_qkv.shape[:2] + (NA_HEADS, NA_HEAD_DIM)
    return rms_norm(q.reshape(shp), q_g), rms_norm(k.reshape(shp), k_g), v.reshape(shp)

def neighbourhood_attention(q, k, v, k_ctx, v_ctx, rpb):
    bsz, n_tok, n_h, d = q.shape
    rows = n_tok // GRID_W
    kh = min(NA_WIN_H, rows)
    r = jnp.arange(rows, dtype=jnp.int32)
    cidx = jnp.arange(GRID_W, dtype=jnp.int32)
    r0 = jnp.clip(r - kh // 2, 0, rows - kh)
    c0 = jnp.clip(cidx - NA_WIN_W // 2, 0, GRID_W - NA_WIN_W)
    row_idx = r0[:, None] + jnp.arange(kh, dtype=jnp.int32)[None, :]
    qg = q.reshape(bsz, rows, GRID_W, n_h, d)
    k_rows = k.reshape(bsz, rows, GRID_W, n_h, d)[:, row_idx]
    v_rows = v.reshape(bsz, rows, GRID_W, n_h, d)[:, row_idx]
    s_loc = jnp.einsum('brqhd,brjkhd->bhrqjk', qg, k_rows).astype(jnp.float32) * NA_SCALE
    dr_idx = row_idx - r[:, None] + (NA_WIN_H - 1)
    dc_idx = jnp.clip(cidx[None, :] - cidx[:, None] + (NA_WIN_W - 1), 0, 2 * NA_WIN_W - 2)
    bias = rpb[:, dr_idx[:, None, :, None], dc_idx[None, :, None, :]]
    in_win = (cidx[None, :] >= c0[:, None]) & (cidx[None, :] < c0[:, None] + NA_WIN_W)
    s_loc = jnp.where(in_win[None, None, None, :, None, :], s_loc + bias[None].astype(jnp.float32), NEG_INF)
    s_ctx = jnp.einsum('brqhd,bkhd->bhrqk', qg, k_ctx).astype(jnp.float32) * NA_SCALE
    n_loc = kh * GRID_W
    s_all = jnp.concatenate([s_loc.reshape(bsz, n_h, rows, GRID_W, n_loc), s_ctx], axis=-1)
    p = jax.nn.softmax(s_all, axis=-1)
    p_loc = p[..., :n_loc].reshape(bsz, n_h, rows, GRID_W, kh, GRID_W).astype(v.dtype)
    p_ctx = p[..., n_loc:].astype(v.dtype)
    o = jnp.einsum('bhrqjk,brjkhd->brqhd', p_loc, v_rows) + jnp.einsum('bhrqk,bkhd->brqhd', p_ctx, v_ctx)
    return o.reshape(bsz, n_tok, n_h, d)

def grouped_moe(h, w_router, b_router, w_gate, w_up, w_down):
    shp = h.shape
    t = h.reshape(-1, D_MODEL)
    n_tok = t.shape[0]
    aff = jax.nn.sigmoid(jnp.dot(t, w_router).astype(jnp.float32))
    sel = (aff + b_router.astype(jnp.float32)).reshape(n_tok, N_GROUPS, EXPERTS_PER_GROUP)
    group_score = jnp.sum(lax.top_k(sel, TOP_K)[0], axis=-1)
    g_idx = jnp.argmax(group_score, axis=-1)
    sel_in_group = jnp.take_along_axis(sel, g_idx[:, None, None], axis=1)[:, 0]
    _, local = lax.top_k(sel_in_group, TOP_K)
    e_idx = g_idx[:, None] * EXPERTS_PER_GROUP + local
    w_sel = jnp.take_along_axis(aff, e_idx, axis=-1)
    w_sel = w_sel / jnp.sum(w_sel, axis=-1, keepdims=True)
    gates = jnp.sum(jax.nn.one_hot(e_idx, N_EXPERTS, dtype=jnp.float32) * w_sel[..., None], axis=1)
    hid = jax.nn.silu(jnp.einsum('td,edf->tef', t, w_gate)) * jnp.einsum('td,edf->tef', t, w_up)
    hid = hid * gates[..., None].astype(hid.dtype)
    return jnp.einsum('tef,efd->td', hid, w_down).reshape(shp)

def mixer_inputs(x, shift, scale, lp):
    h = rms_norm(x, lp['norm1_g']) * (1 + scale) + shift
    proj = jnp.dot(h, lp['w_in'])
    q_lat, ckv_raw, krope, conv_in, na_qkv = jnp.split(proj, IN_SPLITS, axis=-1)
    ckv_n = rms_norm(ckv_raw, lp['kv_a_g'])
    q_mla = mla_queries(q_lat, lp['q_a_g'], lp['w_q_up'], lp['mla_q_norm_g'])
    k_mla, v_mla = mla_keys_values(ckv_n, krope, lp['w_kv_up'], lp['mla_k_norm_g'])
    o_conv = conformer_conv(conv_in, lp['conv_dw_w'], lp['conv_dw_b'], lp['conv_ln_g'], lp['conv_ln_b'])
    q_na, k_na, v_na = na_heads(na_qkv, lp['na_q_norm_g'], lp['na_k_norm_g'])
    return q_mla, k_mla, v_mla, ckv_n, krope, o_conv, q_na, k_na, v_na

def finish_layer(x, o_mla, o_conv, o_na, gate1, shift2, scale2, gate2, lp):
    bsz, n_tok = x.shape[:2]
    mix = jnp.concatenate([o_mla.reshape(bsz, n_tok, MLA_WIDTH), o_conv,
                           o_na.reshape(bsz, n_tok, NA_WIDTH)], axis=-1)
    x = x + gate1 * jnp.dot(mix, lp['w_out'])
    h = rms_norm(x, lp['norm2_g']) * (1 + scale2) + shift2
    return x + gate2 * grouped_moe(h, lp['w_router'], lp['b_router'], lp['w_e_gate'], lp['w_e_up'], lp['w_e_down'])

def setup_inputs(seed: int = 0) -> dict:
    key = jax.random.key(seed)
    ks = jax.random.split(key, 40)
    f32 = jnp.float32

    def nrm(i, shape, scale):
        return jax.random.normal(ks[i], shape, f32) * scale

    def gain(i, shape):
        return 1.0 + 0.05 * jax.random.normal(ks[i], shape, f32)

    return {
        'x_prompt': nrm(0, (BATCH, SEQ, D_MODEL), 1.0),
        'x_sample': nrm(1, (DEC_BATCH, DEC_SEQ, D_MODEL), 1.0),
        'cache_mla_ckv': nrm(2, (DEC_BATCH, DEPTH, PAST_LEN, KV_LORA), 1.0),
        'cache_mla_krope': nrm(3, (DEC_BATCH, DEPTH, PAST_LEN, QK_ROPE), 1.0),
        'cache_na_k': nrm(4, (DEC_BATCH, DEPTH, PAST_LEN, NA_HEADS, NA_HEAD_DIM), 1.0),
        'cache_na_v': nrm(5, (DEC_BATCH, DEPTH, PAST_LEN, NA_HEADS, NA_HEAD_DIM), 1.0),
        'c': nrm(6, (DEC_BATCH, D_MODEL), 1.0),
        'c_ctx': nrm(7, (D_MODEL,), 1.0),
        'w_ada': nrm(8, (DEPTH, D_MODEL, 6 * D_MODEL), 0.5 * D_MODEL ** -0.5),
        'b_ada': nrm(9, (DEPTH, 6 * D_MODEL), 0.02),
        'norm1_g': gain(10, (DEPTH, D_MODEL)),
        'norm2_g': gain(11, (DEPTH, D_MODEL)),
        'w_in': nrm(12, (DEPTH, D_MODEL, IN_COLS), D_MODEL ** -0.5),
        'q_a_g': gain(13, (DEPTH, Q_LORA)),
        'kv_a_g': gain(14, (DEPTH, KV_LORA)),
        'w_q_up': nrm(15, (DEPTH, Q_LORA, MLA_HEADS * QK_HEAD), Q_LORA ** -0.5),
        'w_kv_up': nrm(16, (DEPTH, KV_LORA, MLA_HEADS * (QK_NOPE + V_HEAD)), KV_LORA ** -0.5),
        'mla_q_norm_g': gain(17, (DEPTH, QK_HEAD)),
        'mla_k_norm_g': gain(18, (DEPTH, QK_HEAD)),
        'conv_dw_w': nrm(19, (DEPTH, CONV_K, CONV_CH), CONV_K ** -0.5),
        'conv_dw_b': nrm(20, (DEPTH, CONV_CH), 0.02),
        'conv_ln_g': gain(21, (DEPTH, CONV_CH)),
        'conv_ln_b': nrm(22, (DEPTH, CONV_CH), 0.02),
        'na_q_norm_g': gain(23, (DEPTH, NA_HEAD_DIM)),
        'na_k_norm_g': gain(24, (DEPTH, NA_HEAD_DIM)),
        'na_rpb': nrm(25, (DEPTH, NA_HEADS, 2 * NA_WIN_H - 1, 2 * NA_WIN_W - 1), 0.1),
        'w_out': nrm(26, (DEPTH, MIX_WIDTH, D_MODEL), MIX_WIDTH ** -0.5),
        'w_router': nrm(27, (D_MODEL, N_EXPERTS), D_MODEL ** -0.5),
        'b_router': nrm(28, (N_EXPERTS,), 0.01),
        'w_e_gate': nrm(29, (DEPTH, N_EXPERTS, D_MODEL, EXPERT_FF), D_MODEL ** -0.5),
        'w_e_up': nrm(30, (DEPTH, N_EXPERTS, D_MODEL, EXPERT_FF), D_MODEL ** -0.5),
        'w_e_down': nrm(31, (DEPTH, N_EXPERTS, EXPERT_FF, D_MODEL), EXPERT_FF ** -0.5),
    }

def reference(x_prompt, x_sample, cache_mla_ckv, cache_mla_krope, cache_na_k, cache_na_v, c, c_ctx,
              w_ada, b_ada, norm1_g, norm2_g, w_in, q_a_g, kv_a_g, w_q_up, w_kv_up, mla_q_norm_g,
              mla_k_norm_g, conv_dw_w, conv_dw_b, conv_ln_g, conv_ln_b, na_q_norm_g, na_k_norm_g, na_rpb,
              w_out, w_router, b_router, w_e_gate, w_e_up, w_e_down):
    layers = []
    for l in range(DEPTH):
        layers.append({
            'w_in': w_in[l], 'norm1_g': norm1_g[l], 'norm2_g': norm2_g[l],
            'q_a_g': q_a_g[l], 'kv_a_g': kv_a_g[l], 'w_q_up': w_q_up[l], 'w_kv_up': w_kv_up[l],
            'mla_q_norm_g': mla_q_norm_g[l], 'mla_k_norm_g': mla_k_norm_g[l],
            'conv_dw_w': conv_dw_w[l], 'conv_dw_b': conv_dw_b[l], 'conv_ln_g': conv_ln_g[l], 'conv_ln_b': conv_ln_b[l],
            'na_q_norm_g': na_q_norm_g[l], 'na_k_norm_g': na_k_norm_g[l], 'na_rpb': na_rpb[l],
            'w_out': w_out[l], 'w_router': w_router, 'b_router': b_router,
            'w_e_gate': w_e_gate[l], 'w_e_up': w_e_up[l], 'w_e_down': w_e_down[l],
        })

    xp = x_prompt
    ckv_list, krope_list, nak_list, nav_list = [], [], [], []
    for l in range(DEPTH):
        lp = layers[l]
        sh1, sc1, g1, sh2, sc2, g2 = modulation(c_ctx, w_ada[l], b_ada[l])
        q, k, v, ckv_n, krope, o_conv, qn, kn, vn = mixer_inputs(xp, sh1, sc1, lp)
        o_mla = blocked_attention(q, k, v, MLA_SCALE)
        o_na = blocked_attention(qn, kn, vn, NA_SCALE)
        xp = finish_layer(xp, o_mla, o_conv, o_na, g1, sh2, sc2, g2, lp)
        ckv_list.append(ckv_n)
        krope_list.append(krope)
        nak_list.append(kn)
        nav_list.append(vn)

    xs = x_sample
    cos, sin = axial_rope_tables(x_sample.shape[1])
    for l in range(DEPTH):
        lp = layers[l]
        sh1, sc1, g1, sh2, sc2, g2 = [m[:, None, :] for m in modulation(c, w_ada[l], b_ada[l])]
        q, k, v, _, _, o_conv, qn, kn, vn = mixer_inputs(xs, sh1, sc1, lp)
        q = rotate_tail(q, cos, sin)
        k = rotate_tail(k, cos, sin)
        k_ctx, v_ctx = mla_keys_values(cache_mla_ckv[:, l], cache_mla_krope[:, l], lp['w_kv_up'], lp['mla_k_norm_g'])
        o_mla = blocked_attention(q, jnp.concatenate([k, k_ctx], axis=1), jnp.concatenate([v, v_ctx], axis=1), MLA_SCALE)
        o_na = neighbourhood_attention(qn, kn, vn, cache_na_k[:, l], cache_na_v[:, l], lp['na_rpb'])
        xs = finish_layer(xs, o_mla, o_conv, o_na, g1, sh2, sc2, g2, lp)

    return (xp, xs, jnp.stack(ckv_list, axis=1), jnp.stack(krope_list, axis=1),
            jnp.stack(nak_list, axis=1), jnp.stack(nav_list, axis=1))


_drawn_inputs = setup_inputs


def setup_inputs(seed=0):
    import zlib

    import numpy as np

    out = dict(_drawn_inputs(seed))
    spreads = {}
    factors = {'cache_mla_krope': 3.543,
     'q_a_g': 5.835,
     'mla_q_norm_g': 3.679,
     'mla_k_norm_g': 5.847,
     'conv_ln_b': 4.154,
     'na_q_norm_g': 6.669,
     'na_rpb': 5.854}
    for name, (base, spread) in spreads.items():
        noise = np.random.default_rng([zlib.crc32(name.encode()), seed]).standard_normal(out[name].shape)
        drawn = base * np.exp(spread * noise) if base else spread * noise
        out[name] = __import__('jax').numpy.asarray(drawn.astype(out[name].dtype))
    for name, factor in factors.items():
        out[name] = (out[name] * factor).astype(out[name].dtype)
    return out
```

```python
from contextlib import ExitStack

import concourse.bass as bass
import numpy as np
from concourse import mybir

F32 = mybir.dt.float32
ALU = mybir.AluOpType
ACT = mybir.ActivationFunctionType
AX = mybir.AxisListType.X

P = 128
D_MODEL, DEPTH, GRID_W = 1024, 2, 64
KC = D_MODEL // P
TILES = 3
TOK = TILES * P
HEADS, NOPE, ROPE, VD = 8, 64, 32, 64
QKD = NOPE + ROPE
QL, KVL = 256, 128
CONV_CH, TAPS = 256, 31
NAH, NAD = 4, 64
NE, NG, EPG, TOP_K, FF = 16, 4, 4, 2, 512
FC = FF // P
EPS = 1e-6
MLA_SCALE, NA_SCALE = QKD ** -0.5, NAD ** -0.5
WIN_H, WIN_W = 8, 16
MASKED = -1e30
IN_COLS = QL + KVL + ROPE + 2 * CONV_CH + 3 * NAH * NAD
O_KV, O_KR, O_A, O_G = QL, QL + KVL, QL + KVL + ROPE, QL + KVL + ROPE + CONV_CH
O_NA = O_G + CONV_CH

RING, SLOT = 6, 2048
ADA_SLOTS = 6 * D_MODEL // 256
IN_SLOTS = -(-IN_COLS // 256)
OUT_SLOTS = D_MODEL // 256
S_IN = ADA_SLOTS
S_UP = S_IN + IN_SLOTS
S_OUT = S_UP + 1
S_EXP = S_OUT + OUT_SLOTS
PER_EXPERT = 6
LAYER_SLOTS = S_EXP + NE * PER_EXPERT
LAST_W = IN_COLS - 256 * (IN_SLOTS - 1)
assert S_EXP % RING == 0 and LAYER_SLOTS % RING == 0 and RING == PER_EXPERT

V_ADA, V_N1, V_N2, V_DWB, V_LNG, V_LNB, V_QAG, V_TAP = 0, 48, 56, 64, 66, 68, 70, 72
DVE_STEPS, ACT_STEPS = 225, 7
VEC = V_TAP + 2 * TAPS
R_Q, R_K, R_NQ, R_NK, R_KV = 0, QKD, 2 * QKD, 2 * QKD + NAD, 2 * QKD + 2 * NAD
ROWS = R_KV + KVL

PAD = TAPS // 2
C_CTX, C_LAT = PAD, 2 * PAD + P
C_LEN = 3 * PAD + TOK
C_OUT = C_LEN - 2 * PAD

RMS = ["norm1", "latent", "heads0", "heads1", "heads2", "conv", "norm2"]
GROUPS = [(p, h) for p in range(3) for h in range(4)]

PER_LAYER = dict(
    small_loaded=16 * 5, bias_loaded=16 * 16, na_cache_loaded=16, mod_ready=2, squares_ready=2,
    meansq_ready=len(RMS), rstd_ready=len(RMS), normed_tile=2 * TILES, latents_normed=1,
    gate_sigmoid=1, glu_ready=1, conv_done=1, conv_mixed=1,
    heads_normed=3, negmax_ready=len(GROUPS), na_exp_done=2 * 4, x_mid=TILES, x_done=1,
    latents_stored=16, values_stored=16 * 2, keys_stored=16, dve_step=DVE_STEPS, act_step=ACT_STEPS,
)


def heads_transposed(p):
    return [(kind, p, h) for h in range(4) for kind in ("qT", "kT")]


def psum_plan():
    order = []
    for s in range(ADA_SLOTS):
        order += [("ada", s)]
        if s % 4 == 0 and s:
            order += [("mod", s // 4 - 1)]
    order += [("mod", 5)] + [("n1", c) for c in range(KC)]
    order += [("proj", j, t) for j in range(4) for t in range(TILES)]
    order += [("ql", 0), ("ql", 1), ("ckv",)]
    order += [("proj", 4, t) for t in range(TILES)]
    order += [("conv", 0), ("conv", 1)]
    order += [("q", 0, t) for t in range(3)] + [("kv", 0, t) for t in range(4)]
    order += [("proj", j, t) for j in (5, 6) for t in range(TILES)]
    order += heads_transposed(0)
    order += [("q", 1, t) for t in range(3)] + [("kv", 1, t) for t in range(4)]
    for i in range(len(GROUPS) + 2):
        if i < len(GROUPS):
            order += [("S", i, t) for t in range(3)]
        if 1 <= i <= len(GROUPS):
            order += [("PT", i - 1, 0), ("PT", i - 1, 1)]
        if i >= 2:
            order += [("O", i - 2)]
        if i == 1:
            order += heads_transposed(1)
        if i == 5:
            order += heads_transposed(2)
        if i == 9:
            order += [("cb", t) for t in range(3)]
        if i == 10:
            order += [("ln", 0), ("ln", 1)]
    order += [("g1", c, n) for c in range(2) for n in range(2)]
    order += [("mix", c) for c in range(6)]
    order += [("out", j, t) for j in range(OUT_SLOTS) for t in range(3)]
    order += [("n2", c) for c in range(KC)] + [("router",)]
    order += [("g2", c, n) for c in range(2) for n in range(2)]
    return {name: n for n, name in enumerate(order)}


def expert_plan():
    order = [("G", t) for t in range(TILES)] + [("U", t) for t in range(TILES)]
    for t in range(TILES):
        order += [("T", t), ("Y", t, 0), ("Y", t, 1)]
    return {name: n for n, name in enumerate(order)}


PLAN, EXPERT = psum_plan(), expert_plan()
BANKS = 8
SPARE = -len(PLAN) % BANKS
LEAD = (len(PLAN) + SPARE) // BANKS
PER_E = (len(EXPERT) + 1) // BANKS
assert len(EXPERT) + 1 == PER_E * BANKS
TURNS = LEAD + NE * PER_E


def build(nc, wring, x_in, vec, rows, ckv_cache, kr_cache, nak_cache, nav_cache, cond, w_router,
          b_router, rope, ident, na_mask, na_bias,
          y_prompt, y_sample, new_ckv, new_krope, new_nak, new_nav):
    with ExitStack() as ctx:
        def sb(name, *shape):
            return ctx.enter_context(nc.sbuf_tensor(name, list(shape), F32))

        def sem(name):
            return ctx.enter_context(nc.semaphore(name))

        ring = sb("ring", P, RING, SLOT)
        x = sb("x", P, TILES, D_MODEL)
        hT = sb("hT", P, KC, TOK)
        xn = sb("xn", P, TILES, D_MODEL)
        proj = sb("proj", P, TILES, IN_COLS)
        v_mla = sb("v_mla", P, 4, HEADS, VD)
        qT = sb("qT", P, 2, 4, TOK)
        kT = sb("kT", P, 2, 4, TOK + P)
        qk = sb("qk", P, 7, 4, QKD)
        squares = sb("squares", P, 1536)
        probs = sb("probs", P, 2, 7 * P)
        probsT = sb("probsT", P, 2, 7 * P)
        biased = sb("biased", P, 2, 2, TOK)
        bias = sb("bias", P, 2, NAH, 2 * P)
        conv_in = sb("conv_in", P, 2, C_LEN)
        conv_acc = sb("conv_acc", P, 2, C_OUT)
        qlatT = sb("qlatT", P, 2, TOK)
        ckvT = sb("ckvT", P, TOK + P)
        ckvn = sb("ckvn", P, TILES, KVL)
        modT = sb("modT", P, 6, KC, 2)
        a1 = sb("a1", P, KC, 2)
        a2 = sb("a2", P, KC, 2)
        vecs = sb("vecs", P, VEC)
        rowv = sb("rowv", P, ROWS)
        krc = sb("krc", P, ROPE)
        nav = sb("nav", P, NAH, NAD)
        condT = sb("condT", P, KC, 2)
        cond_e = sb("cond_e", P, KC, 2)
        wr = sb("wr", P, KC, NE)
        br = sb("br", P, NE)
        ropes = sb("ropes", P, 2, 2, ROPE)
        iden = sb("iden", P, P)
        mask = sb("mask", P, GRID_W)
        ssum = sb("ssum", P, 32)
        ms = sb("ms", P, 32)
        lnb = sb("lnb", P, 32)
        rstd = sb("rstd", P, 32)
        stats = sb("stats", P, TILES, 6)
        meanvar = sb("meanvar", P, TILES, 2)
        negmax = sb("negmax", P, 12, 3)
        rowmax = sb("rowmax", P, 3)
        rowsum = sb("rowsum", P, 12, 3)
        turned = sb("turned", P, 2, 2 * 4 * ROPE)
        aff = sb("aff", P, TILES * NE)
        sel = sb("sel", P, TILES * NE)
        gates = sb("gates", P, TILES, NE)
        tiew = sb("tiew", P, NG)
        bank = [ctx.enter_context(nc.psum_tensor(f"bank{i}", [P, 512], F32)) for i in range(BANKS)]

        modrow = qT[0:2, :, :, :].rearrange("p a h n -> p (a h n)")[:, 0:2048].rearrange("p (b n) -> p b n", b=2)
        G = kT[:, 1, :, :].rearrange("p h n -> p (h n)").rearrange("p (c n) -> p c n", c=2)
        acc = proj[:, :, 0:D_MODEL]
        sg = probs[:, :, :].rearrange("p a n -> p (a n)")[:, 0:TILES * FF].rearrange("p (t n) -> p t n", t=TILES)
        hid = qT[:, :, :, :].rearrange("p a h n -> p (a h n)")[:, 0:TILES * FF].rearrange("p (t n) -> p t n", t=TILES)
        hidT = probsT[:, :, :].rearrange("p a n -> p (a n)")[:, 0:TILES * FF].rearrange("p (t n) -> p t n", t=TILES)
        q_lat_n = probsT[:, 0, 0:TILES * QL].rearrange("p (t n) -> p t n", t=TILES)
        glu = probs[:, 0, 0:TILES * CONV_CH].rearrange("p (t n) -> p t n", t=TILES)
        ln_tm = squares[:, 0:TILES * CONV_CH].rearrange("p (t n) -> p t n", t=TILES)
        z_conv = squares[:, CONV_CH * TILES:2 * CONV_CH * TILES].rearrange("p (c n) -> p c n", c=2)
        rt = biased[:, 0, 0, 0:6 * TILES * NE].rearrange("p (a n) -> p a n", a=6)
        gated = biased[:, :, :, :].rearrange("p a b n -> p (a b n)")

        sems = {name: sem(name) for name in PER_LAYER}
        consts_loaded, consts_made = sem("consts_loaded"), sem("consts_made")
        cond_exp, cond_ready = sem("cond_exp"), sem("cond_ready")
        carried = sem("carried")
        slot_full = [sem(f"slot_full{i}") for i in range(RING)]
        slot_free = [sem(f"slot_free{i}") for i in range(RING)]
        bank_full = [sem(f"bank_full{i}") for i in range(BANKS)]
        bank_read = [sem(f"bank_read{i}") for i in range(BANKS)]
        outputs_stored = sem("outputs_stored")
        N_CONST = 16 * 7

        def nth(l, name, k):
            return l * PER_LAYER[name] + k

        def bank_no(key, e=None):
            return (PLAN[key] if e is None else EXPERT[key]) % BANKS

        def turns_before(l, key, e=None):
            if e is None:
                return l * TURNS + PLAN[key] // BANKS
            return l * TURNS + (e * PER_E + (LEAD + EXPERT[key] // BANKS))

        def once_free(l, key, e=None):
            return bank_read[bank_no(key, e)], turns_before(l, key, e) + 1

        def once_full(l, key, e=None):
            return bank_full[bank_no(key, e)], turns_before(l, key, e) + 1

        def once_read(l, key, e=None):
            return bank_read[bank_no(key, e)], turns_before(l, key, e) + 2

        def once_loaded(l, s):
            return slot_full[s % RING], l * (16 * LAYER_SLOTS // RING) + 16 * (s // RING + 1)

        def middle(ap, n):
            return ap.unsqueeze(2).broadcast_to([ap.shape[0], ap.shape[1], n, ap.shape[2]])

        def last(ap, n):
            return ap.unsqueeze(len(ap.shape)).broadcast_to(list(ap.shape) + [n])

        block = ctx.enter_context(nc.Block())

        @block.sync
        def _(sp):
            for i in range(RING):
                sp.sem_inc(slot_free[i], 1)
            with sp.Fori(0, DEPTH * LAYER_SLOTS // RING) as n:
                for i in range(RING):
                    sp.wait_ge(slot_free[i], n + 1)
                    sp.dma_start(ring[:, i, :], wring[bass.ds(n * RING + i, 1)].rearrange("o p n -> (o p) n")) \
                      .then_inc(slot_full[i], 16)

        @block.gpsimd
        def _(pool):

            pool.dma_start(x[:], x_in).then_inc(consts_loaded, 16)
            pool.dma_start(condT[:], cond).then_inc(consts_loaded, 16)
            pool.dma_start(iden[:], ident).then_inc(consts_loaded, 16)
            pool.dma_start(wr[:], w_router).then_inc(consts_loaded, 16)
            pool.dma_start(br[:], b_router.partition_broadcast(P)).then_inc(consts_loaded, 16)
            pool.dma_start(ropes[:], rope).then_inc(consts_loaded, 16)
            pool.dma_start(mask[:], na_mask).then_inc(consts_loaded, 16)
            pool.memset(conv_in[:], 0.0).then_inc(consts_made, 1)
            for g in range(NG):
                pool.memset(tiew[:, g:g + 1], float(NG - g)).then_inc(consts_made, 1)
            pool.sem_inc(sems["x_done"], 1)
            with pool.Fori(0, DEPTH) as l:
                lay = bass.ds(l, 1)
                pool.wait_ge(sems["x_done"], nth(l, "x_done", 1))
                pool.sem_inc(carried, 1)
                pool.dma_start(vecs[:], vec[lay].rearrange("o p n -> (o p) n")).then_inc(sems["small_loaded"], 16)
                pool.dma_start(rowv[:], rows[lay].rearrange("o n -> (o n)").partition_broadcast(P)) \
                    .then_inc(sems["small_loaded"], 16)
                pool.dma_start(ckvT[:, TOK:TOK + P], ckv_cache[lay].rearrange("o p n -> (o p) n")) \
                    .then_inc(sems["small_loaded"], 16)
                pool.dma_start(krc[:], kr_cache[lay].rearrange("o p n -> (o p) n")).then_inc(sems["small_loaded"], 16)
                pool.dma_start(nav[:], nav_cache[lay].rearrange("o p h n -> (o p) h n")) \
                    .then_inc(sems["small_loaded"], 16)
                for t in range(2):
                    for r in range(2):
                        first = WIN_H - 1 - (2 * t + r)
                        for h in range(NAH):
                            pool.dma_start(bias[r * GRID_W:(r + 1) * GRID_W, t, h, :].rearrange("q (j k) -> q j k", k=GRID_W), na_bias[lay, :, h, first:first + 4, :].rearrange("o q j k -> (o q) j k")) \
                                .then_inc(sems["bias_loaded"], 16)
                pool.wait_ge(sems["latents_normed"], nth(l, "latents_normed", 1))
                pool.sem_inc(carried, 1)
                pool.dma_start(new_ckv[lay].rearrange("o p n -> (o p) n"), ckvn[:, 0, :]) \
                    .then_inc(sems["latents_stored"], 16)
                pool.wait_ge(*once_read(l, ("proj", 6, 0)))
                pool.sem_inc(carried, 1)
                pool.dma_start(new_krope[lay].rearrange("o p n -> (o p) n"), proj[:, 0, O_KR:O_KR + ROPE]) \
                    .then_inc(sems["values_stored"], 16)
                pool.dma_start(new_nav[lay].rearrange("o p n -> (o p) n"), proj[:, 0, O_NA + 512:O_NA + 768]) \
                    .then_inc(sems["values_stored"], 16)
                pool.wait_ge(sems["heads_normed"], nth(l, "heads_normed", 3))
                pool.sem_inc(carried, 1)
                pool.dma_start(new_nak[lay].rearrange("o p (h n) -> (o p) h n", h=NAH), qk[:, 3, :, 0:NAD]) \
                    .then_inc(sems["keys_stored"], 16)
                pool.wait_ge(*once_full(l, ("S", 4, 0)))
                pool.sem_inc(carried, 1)
                pool.dma_start(kT[0:NAD, 0, :, TOK:TOK + P], nak_cache[lay].rearrange("o p h n -> (o p) h n")) \
                    .then_inc(sems["na_cache_loaded"], 16)
                for name in ("latents_stored", "values_stored", "keys_stored"):
                    pool.wait_ge(sems[name], nth(l, name, PER_LAYER[name]))
            pool.wait_ge(sems["x_done"], DEPTH + 1)
            pool.dma_start(y_prompt, x[:, 0, :]).then_inc(outputs_stored, 16)
            pool.dma_start(y_sample.rearrange("(t p) n -> p t n", p=P), x[:, 1:3, :]).then_inc(outputs_stored, 16)
            pool.wait_ge(outputs_stored, 32)

        @block.tensor
        def _(pe):

            def pass_over(n):
                pe.sem_inc(bank_full[n % BANKS], 1)
                pe.sem_inc(bank_read[n % BANKS], 1)


            def turn_around(l, key, parts, d=P, frees_slot=None):
                pe.wait_ge(*once_free(l, key))
                b = bank[bank_no(key)]
                if d == NAD:
                    pe.sem_inc(carried, 1)
                for i, part in enumerate(parts):
                    mm = pe.transpose(b[0:d, i * P:(i + 1) * P], part, iden[:])
                    if i == 0 and frees_slot is not None:
                        mm.then_inc(slot_free[frees_slot % RING], 1)
                mm.then_inc(bank_full[bank_no(key)], 1)

            def project(l, j, frees_slot=None):
                n = 256 if j < IN_SLOTS - 1 else LAST_W
                pe.wait_ge(*once_loaded(l, S_IN + j))
                w = ring[:, (S_IN + j) % RING, :][:, 0:KC * n].rearrange("p (k n) -> p k n", k=KC)
                for t in range(TILES):
                    pe.wait_ge(*once_free(l, ("proj", j, t)))
                    b = bank[bank_no(("proj", j, t))]
                    for c in range(KC):
                        mm = pe.matmul(b[:, 0:n], hT[:, c, t * P:(t + 1) * P], w[:, c, :],
                                       start=(c == 0), stop=(c == KC - 1))
                        if c == 0 and t == 0 and frees_slot is not None:
                            mm.then_inc(slot_free[frees_slot % RING], 1)
                    mm.then_inc(bank_full[bank_no(("proj", j, t))], 1)

            def queries(l, p):
                pe.wait_ge(*once_loaded(l, S_UP))
                w = ring[:, S_UP % RING, :][:, 0:2 * 768].rearrange("p (k n) -> p k n", k=2)
                for t in range(TILES):
                    pe.wait_ge(*once_free(l, ("q", p, t)))
                    b = bank[bank_no(("q", p, t))]
                    for c in range(2):
                        mm = pe.matmul(b[:, 0:384], qlatT[:, c, t * P:(t + 1) * P], w[:, c, p * 384:(p + 1) * 384],
                                       start=(c == 0), stop=(c == 1))
                    mm.then_inc(bank_full[bank_no(("q", p, t))], 1)

            def keys_values(l, p):
                if p == 0:
                    pe.wait_ge(*once_loaded(l, S_UP))
                    w = ring[:, S_UP % RING, :][:, 1536:2048]
                else:
                    pe.wait_ge(*once_loaded(l, S_UP - 1))
                    w = ring[:, (S_UP - 1) % RING, :][:, KC * LAST_W:KC * LAST_W + 512]
                for t in range(4):
                    pe.wait_ge(*once_free(l, ("kv", p, t)))
                    b = bank[bank_no(("kv", p, t))]
                    mm = pe.matmul(b[:, :], ckvT[:, t * P:(t + 1) * P], w, start=True, stop=True)
                    mm.then_inc(bank_full[bank_no(("kv", p, t))], 1)

            def turn_heads(l, p):
                d = QKD if p < 2 else NAD
                pe.wait_ge(sems["heads_normed"], nth(l, "heads_normed", p + 1))
                for h in range(4):
                    turn_around(l, ("qT", p, h), [qk[:, t, h, 0:d] for t in range(3)], d)
                    turn_around(l, ("kT", p, h), [qk[:, 3 + t, h, 0:d] for t in range(4 if p < 2 else 3)], d)

            def scores(l, g):
                p, h = GROUPS[g]
                d, s = (QKD if p < 2 else NAD), p % 2
                pe.wait_ge(*once_read(l, ("qT", p, h)))
                pe.wait_ge(*once_read(l, ("kT", p, h)))
                if g == 8:
                    pe.wait_ge(sems["na_cache_loaded"], nth(l, "na_cache_loaded", 16))
                for t in range(TILES):
                    pe.wait_ge(*once_free(l, ("S", g, t)))
                    b = bank[bank_no(("S", g, t))]
                    lo, hi = (0, P) if t == 0 else (P, 4 * P)
                    mm = pe.matmul(b[:, 0:hi - lo], qT[0:d, s, h, t * P:(t + 1) * P], kT[0:d, s, h, lo:hi],
                                   start=True, stop=True)
                    mm.then_inc(bank_full[bank_no(("S", g, t))], 1)

            def turn_probs(l, g):
                if GROUPS[g][0] < 2:
                    pe.wait_ge(*once_read(l, ("S", g, 2)))
                else:
                    pe.wait_ge(sems["na_exp_done"], nth(l, "na_exp_done", 2 * GROUPS[g][1] + 2))
                part = [probs[:, g % 2, k * P:(k + 1) * P] for k in range(7)]
                pe.wait_ge(*once_free(l, ("PT", g, 0)))
                b = bank[bank_no(("PT", g, 0))]
                for k in range(4):
                    mm = pe.transpose(b[:, k * P:(k + 1) * P], part[k], iden[:])
                    if g == 0 and k < 2:
                        mm.then_inc(slot_free[(S_UP - 1 + k) % RING], 1)
                mm.then_inc(bank_full[bank_no(("PT", g, 0))], 1)
                turn_around(l, ("PT", g, 1), part[4:])

            def values(l, g):
                p, h = GROUPS[g]
                pe.wait_ge(*once_read(l, ("PT", g, 0)))
                pe.wait_ge(*once_read(l, ("PT", g, 1)))
                pe.wait_ge(*once_free(l, ("O", g)))
                b = bank[bank_no(("O", g))]
                for t in range(TILES):
                    keys = [0] if t == 0 else [1, 2, 3]
                    for i, k in enumerate(keys):
                        col = 0 if t == 0 else 1 + 3 * (t - 1) + i
                        if p < 2:
                            v = v_mla[:, k, 4 * p + h, :]
                        elif k == 3:
                            v = nav[:, h, :]
                        else:
                            v = proj[:, k, O_NA + 512 + h * NAD:O_NA + 512 + (h + 1) * NAD]
                        mm = pe.matmul(b[:, t * VD:(t + 1) * VD], probsT[:, g % 2, col * P:(col + 1) * P], v,
                                       start=(i == 0), stop=(i == len(keys) - 1))
                mm.then_inc(bank_full[bank_no(("O", g))], 1)

            def gate_rows(l, what, m):
                for c in range(2):
                    for n in range(2):
                        pe.wait_ge(*once_free(l, (what, c, n)))
                        b = bank[bank_no((what, c, n))]
                        for i in range(4):
                            mm = pe.matmul(b[:, i * P:(i + 1) * P],
                                           modT[:, m, 4 * n + i, c:c + 1].broadcast_to([P, P]),
                                           iden[:], start=True, stop=True)
                        mm.then_inc(bank_full[bank_no((what, c, n))], 1)

            def turn_mod(l, m):
                pe.wait_ge(*once_read(l, ("ada", 4 * m + 3)))
                pe.wait_ge(*once_free(l, ("mod", m)))
                b = bank[bank_no(("mod", m))]
                pe.sem_inc(carried, 1)
                for c in range(KC):
                    mm = pe.transpose(b[:, 2 * c:2 * c + 2], modrow[:, m % 2, c * P:(c + 1) * P], iden[0:2, 0:2])
                mm.then_inc(bank_full[bank_no(("mod", m))], 1)

            for i in range(BANKS):
                pe.sem_inc(bank_read[i], 1)
            pe.wait_ge(consts_loaded, N_CONST)
            pe.wait_ge(cond_ready, 1)
            with pe.Fori(0, DEPTH) as l:
                for s in range(ADA_SLOTS):
                    pe.wait_ge(*once_loaded(l, s))
                    w = ring[:, s % RING, :].rearrange("p (k n) -> p k n", k=KC)
                    pe.wait_ge(*once_free(l, ("ada", s)))
                    b = bank[bank_no(("ada", s))]
                    for c in range(KC):
                        mm = pe.matmul(b[0:2, 0:256], condT[:, c, :], w[:, c, :], start=(c == 0), stop=(c == KC - 1))
                        if c == 0 and s:
                            mm.then_inc(slot_free[(s - 1) % RING], 1)
                    mm.then_inc(bank_full[bank_no(("ada", s))], 1)
                    if s % 4 == 0 and s:
                        turn_mod(l, s // 4 - 1)
                turn_mod(l, 5)
                pe.wait_ge(sems["normed_tile"], nth(l, "normed_tile", TILES))
                for c in range(KC):
                    turn_around(l, ("n1", c), [xn[:, t, c * P:(c + 1) * P] for t in range(TILES)],
                                frees_slot=ADA_SLOTS - 1 if c == 0 else None)
                pe.wait_ge(*once_read(l, ("n1", 6)))
                pe.wait_ge(*once_read(l, ("n1", 7)))
                for j in range(4):
                    project(l, j, S_IN + j - 1 if j else None)
                pe.wait_ge(sems["latents_normed"], nth(l, "latents_normed", 1))
                for c in range(2):
                    turn_around(l, ("ql", c), [q_lat_n[:, t, c * P:(c + 1) * P] for t in range(TILES)],
                                frees_slot=S_IN + 3 if c == 0 else None)
                turn_around(l, ("ckv",), [ckvn[:, t, :] for t in range(TILES)])
                project(l, 4)
                pe.wait_ge(sems["glu_ready"], nth(l, "glu_ready", 1))
                for c in range(2):
                    turn_around(l, ("conv", c), [glu[:, t, c * P:(c + 1) * P] for t in range(TILES)],
                                frees_slot=S_IN + 4 if c == 0 else None)
                pe.wait_ge(*once_read(l, ("ql", 1)))
                pe.wait_ge(*once_read(l, ("ckv",)))
                pe.wait_ge(sems["small_loaded"], nth(l, "small_loaded", PER_LAYER["small_loaded"]))
                queries(l, 0)
                keys_values(l, 0)
                project(l, 5)
                project(l, 6, S_IN + 5)
                turn_heads(l, 0)
                queries(l, 1)
                keys_values(l, 1)
                for i in range(len(GROUPS) + 2):
                    if i < len(GROUPS):
                        scores(l, i)
                    if 1 <= i <= len(GROUPS):
                        turn_probs(l, i - 1)
                    if i >= 2:
                        values(l, i - 2)
                    if i == 1:
                        turn_heads(l, 1)
                    if i == 5:
                        turn_heads(l, 2)
                    if i == 9:
                        pe.wait_ge(sems["conv_done"], nth(l, "conv_done", 1))
                        for t in range(TILES):
                            at = 0 if t == 0 else C_LAT - PAD + (t - 1) * P
                            turn_around(l, ("cb", t), [conv_acc[:, c, at:at + P] for c in range(2)])
                    if i == 10:
                        pe.wait_ge(*once_read(l, ("cb", 2)))
                        for c in range(2):
                            turn_around(l, ("ln", c), [ln_tm[:, t, c * P:(c + 1) * P] for t in range(TILES)])
                gate_rows(l, "g1", 2)
                pe.wait_ge(*once_read(l, ("O", len(GROUPS) - 1)))
                for c in range(6):
                    turn_around(l, ("mix", c), [xn[:, t, c * P:(c + 1) * P] for t in range(TILES)])
                pe.wait_ge(*once_read(l, ("mix", 5)))
                pe.wait_ge(sems["conv_mixed"], nth(l, "conv_mixed", 1))
                for j in range(OUT_SLOTS):
                    pe.wait_ge(*once_loaded(l, S_OUT + j))
                    w = ring[:, (S_OUT + j) % RING, :].rearrange("p (k n) -> p k n", k=KC)
                    for t in range(TILES):
                        pe.wait_ge(*once_free(l, ("out", j, t)))
                        b = bank[bank_no(("out", j, t))]
                        for c in range(KC):
                            mm = pe.matmul(b[:, 0:256], hT[:, c, t * P:(t + 1) * P], w[:, c, :],
                                           start=(c == 0), stop=(c == KC - 1))
                            if j and t == 0 and c == 0:
                                mm.then_inc(slot_free[(S_OUT + j - 1) % RING], 1)
                        mm.then_inc(bank_full[bank_no(("out", j, t))], 1)
                pe.wait_ge(sems["normed_tile"], nth(l, "normed_tile", 2 * TILES))
                for c in range(KC):
                    turn_around(l, ("n2", c), [xn[:, t, c * P:(c + 1) * P] for t in range(TILES)],
                                frees_slot=S_EXP - 1 if c == 0 else None)
                pe.wait_ge(*once_read(l, ("n2", 6)))
                pe.wait_ge(*once_read(l, ("n2", 7)))
                pe.wait_ge(*once_free(l, ("router",)))
                b = bank[bank_no(("router",))]
                for t in range(TILES):
                    for c in range(KC):
                        mm = pe.matmul(b[:, t * NE:(t + 1) * NE], hT[:, c, t * P:(t + 1) * P], wr[:, c, :],
                                       start=(c == 0), stop=(c == KC - 1))
                mm.then_inc(bank_full[bank_no(("router",))], 1)
                gate_rows(l, "g2", 5)
                for n in range(SPARE):
                    pass_over(len(PLAN) + n)
                with pe.Fori(0, NE) as e:
                    loads = l * (16 * LAYER_SLOTS // RING) + (e * 16 + 16 * (S_EXP // RING + 1))
                    for what, s in (("G", 0), ("U", 2)):
                        pe.wait_ge(slot_full[s], loads)
                        pe.wait_ge(slot_full[s + 1], loads)
                        w = [ring[:, s + i, :].rearrange("p (k n) -> p k n", k=4) for i in range(2)]
                        for t in range(TILES):
                            pe.wait_ge(*once_free(l, (what, t), e))
                            b = bank[bank_no((what, t), e)]
                            for c in range(KC):
                                mm = pe.matmul(b[:, :], hT[:, c, t * P:(t + 1) * P], w[c // 4][:, c % 4, :],
                                               start=(c == 0), stop=(c == KC - 1))
                                if t == TILES - 1 and c == 3:
                                    mm.then_inc(slot_free[s % RING], 1)
                                if s == 2 and t == 0 and c == 0:
                                    mm.then_inc(slot_free[1 % RING], 1)
                            mm.then_inc(bank_full[bank_no((what, t), e)], 1)
                    pe.wait_ge(slot_full[4], loads)
                    pe.wait_ge(slot_full[5], loads)
                    w = [ring[:, 4 + i, :].rearrange("p (k n) -> p k n", k=2) for i in range(2)]
                    for t in range(TILES):
                        pe.wait_ge(*once_read(l, ("U", t), e))
                        pe.wait_ge(*once_free(l, ("T", t), e))
                        b = bank[bank_no(("T", t), e)]
                        for c in range(FC):
                            mm = pe.transpose(b[:, c * P:(c + 1) * P], hid[:, t, c * P:(c + 1) * P], iden[:])
                            if t == 0 and c == 0:
                                mm.then_inc(slot_free[3 % RING], 1)
                        mm.then_inc(bank_full[bank_no(("T", t), e)], 1)
                        pe.wait_ge(*once_read(l, ("T", t), e))
                        y = []
                        for n in range(2):
                            pe.wait_ge(*once_free(l, ("Y", t, n), e))
                            y.append(bank[bank_no(("Y", t, n), e)])
                        for c in range(FC):
                            for n in range(2):
                                mm = pe.matmul(y[n][:, :], hidT[:, t, c * P:(c + 1) * P],
                                               w[c // 2][:, c % 2, n * 512:(n + 1) * 512],
                                               start=(c == 0), stop=(c == FC - 1))
                                if c == FC - 1:
                                    mm.then_inc(bank_full[bank_no(("Y", t, n), e)], 1)
                                if t == TILES - 1 and c == 1 and n == 1:
                                    mm.then_inc(slot_free[4 % RING], 1)
                    n = len(EXPERT)
                    pe.wait_ge(bank_read[n % BANKS], l * TURNS + (e * PER_E + (LEAD + n // BANKS + 1)))
                    mm = pe.matmul(bank[n % BANKS][0:2, 0:2], condT[:, 0, :], condT[:, 0, :], start=True, stop=True)
                    mm.then_inc(slot_free[5 % RING], 1)
                    pass_over(n)

        @block.scalar
        def _(act):
            count = [0]

            def step(l):
                count[0] += 1
                return nth(l, "act_step", count[0])

            def root(l, name, n):
                act.wait_ge(sems["meansq_ready"], nth(l, "meansq_ready", RMS.index(name) + 1))
                act.activation(lnb[:, 0:n], ms[:, 0:n], ACT.Ln).then_inc(sems["act_step"], 1)
                act.wait_ge(sems["act_step"], step(l))
                act.activation(rstd[:, 0:n], lnb[:, 0:n], ACT.Exp, scale=-0.5).then_inc(sems["rstd_ready"], 1)

            def square_sums(l, k):
                for t in range(TILES):
                    ins = act.activation(xn[:, t, :], x[:, t, :], ACT.Square, accum_out=ssum[:, t:t + 1])
                ins.then_inc(sems["squares_ready"], 1)

            def modulate(l, what, a, m):
                for c in range(1, KC, 2):
                    act.wait_ge(*once_full(l, (what, c)))
                    b = bank[bank_no((what, c))]
                    for q, (lo, hi) in enumerate(((0, P), (P, TOK))):
                        ins = act.activation(hT[:, c, lo:hi], b[:, lo:hi], ACT.Identity,
                                             bias=modT[:, m, c, q:q + 1], scale=a[:, c, q:q + 1])
                    ins.then_inc(bank_read[bank_no((what, c))], 1)

            def evac_proj(l, j):
                n = 256 if j < IN_SLOTS - 1 else LAST_W
                for t in range(TILES):
                    act.wait_ge(*once_full(l, ("proj", j, t)))
                    b = bank[bank_no(("proj", j, t))]
                    act.copy(proj[:, t, j * 256:j * 256 + n], b[:, 0:n]) \
                        .then_inc(bank_read[bank_no(("proj", j, t))], 1)

            def evac_heads(l, p):
                for t in range(TILES):
                    act.wait_ge(*once_full(l, ("q", p, t)))
                    b = bank[bank_no(("q", p, t))]
                    act.copy(qk[:, t, :, :].rearrange("p h n -> p (h n)"), b[:, 0:384]) \
                        .then_inc(bank_read[bank_no(("q", p, t))], 1)
                for t in range(4):
                    act.wait_ge(*once_full(l, ("kv", p, t)))
                    b = bank[bank_no(("kv", p, t))][:, :].rearrange("p (h n) -> p h n", h=4)
                    act.copy(v_mla[:, t, 4 * p:4 * p + 4, :], b[:, :, NOPE:])
                    act.copy(qk[:, 3 + t, :, 0:NOPE], b[:, :, 0:NOPE]).then_inc(bank_read[bank_no(("kv", p, t))], 1)

            def evac_turned(l, p):
                d, s = (QKD if p < 2 else NAD), p % 2
                for h in range(4):
                    act.wait_ge(*once_full(l, ("qT", p, h)))
                    b = bank[bank_no(("qT", p, h))]
                    act.copy(qT[0:d, s, h, :], b[0:d, 0:TOK]).then_inc(bank_read[bank_no(("qT", p, h))], 1)
                    n = 4 * P if p < 2 else TOK
                    act.wait_ge(*once_full(l, ("kT", p, h)))
                    b = bank[bank_no(("kT", p, h))]
                    act.copy(kT[0:d, s, h, 0:n], b[0:d, 0:n]).then_inc(bank_read[bank_no(("kT", p, h))], 1)

            def exponentials(l, g):
                p, h = GROUPS[g]
                act.wait_ge(sems["negmax_ready"], nth(l, "negmax_ready", g + 1))
                for t in range(TILES):
                    lo, hi = (0, P) if t == 0 else (P + (t - 1) * TOK, P + t * TOK)
                    out = probs[:, g % 2, lo:hi]
                    if p == 2 and t:
                        act.activation(out, biased[:, g % 2, t - 1, :], ACT.Exp, bias=negmax[:, g, t:t + 1],
                                       accum_out=rowsum[:, g, t:t + 1]).then_inc(sems["na_exp_done"], 1)
                    else:
                        act.wait_ge(*once_full(l, ("S", g, t)))
                        b = bank[bank_no(("S", g, t))]
                        act.activation(out, b[:, 0:hi - lo], ACT.Exp, bias=negmax[:, g, t:t + 1],
                                             scale=MLA_SCALE if p < 2 else 1.0,
                                             accum_out=rowsum[:, g, t:t + 1]) \
                                                 .then_inc(bank_read[bank_no(("S", g, t))], 1)

            def evac_probs(l, g):
                act.wait_ge(*once_full(l, ("PT", g, 1)))
                b = bank[bank_no(("PT", g, 1))]
                act.copy(probsT[:, g % 2, 4 * P:7 * P], b[:, 0:TOK]).then_inc(bank_read[bank_no(("PT", g, 1))], 1)

            def evac_gates(l, what):
                for c in range(2):
                    for n in range(2):
                        act.wait_ge(*once_full(l, (what, c, n)))
                        b = bank[bank_no((what, c, n))]
                        act.copy(G[:, c, n * 512:(n + 1) * 512], b[:, :]) \
                            .then_inc(bank_read[bank_no((what, c, n))], 1)

            act.wait_ge(consts_loaded, N_CONST)
            act.activation(cond_e[:], condT[:], ACT.Exp, scale=-1.0).then_inc(cond_exp, 1)
            with act.Fori(0, DEPTH) as l:
                count[0] = 0
                act.wait_ge(sems["x_done"], nth(l, "x_done", 1))
                square_sums(l, 1)
                for s in range(ADA_SLOTS):
                    if s % 4 == 0 and s >= 8:
                        act.wait_ge(*once_full(l, ("mod", s // 4 - 2)))
                    act.wait_ge(*once_full(l, ("ada", s)))
                    b = bank[bank_no(("ada", s))]
                    act.copy(modrow[:, (s // 4) % 2, (s % 4) * 256:(s % 4 + 1) * 256], b[0:2, 0:256]) \
                        .then_inc(bank_read[bank_no(("ada", s))], 1)
                    if s == 3:
                        root(l, "norm1", TILES)
                act.wait_ge(sems["mod_ready"], nth(l, "mod_ready", 2))
                modulate(l, "n1", a1, 0)
                for j in range(2):
                    evac_proj(l, j)
                root(l, "latent", 6)
                for j in range(2, 4):
                    evac_proj(l, j)
                act.wait_ge(*once_read(l, ("proj", 3, 2)))
                act.activation(proj[:, :, O_G:O_G + CONV_CH], proj[:, :, O_G:O_G + CONV_CH], ACT.Sigmoid) \
                    .then_inc(sems["gate_sigmoid"], 1)
                evac_proj(l, 4)
                evac_heads(l, 0)
                evac_proj(l, 5)
                root(l, "heads0", 28)
                evac_proj(l, 6)
                evac_turned(l, 0)
                evac_heads(l, 1)
                root(l, "heads1", 28)
                for i in range(len(GROUPS) + 2):
                    if i == 4:
                        root(l, "heads2", 24)
                    if i == 10:
                        root(l, "conv", TILES)
                    if i < len(GROUPS):
                        exponentials(l, i)
                    if 1 <= i <= len(GROUPS):
                        evac_probs(l, i - 1)
                    if i == 1:
                        evac_turned(l, 1)
                    if i == 5:
                        evac_turned(l, 2)
                evac_gates(l, "g1")
                for c in range(6):
                    act.wait_ge(*once_full(l, ("mix", c)))
                    b = bank[bank_no(("mix", c))]
                    act.copy(hT[:, c if c < 4 else c + 2, :], b[:, 0:TOK]).then_inc(bank_read[bank_no(("mix", c))], 1)
                act.wait_ge(*once_read(l, ("ln", 1)))
                act.activation(hT[:, 4:6, :], z_conv, ACT.Silu).then_inc(sems["conv_mixed"], 1)
                act.wait_ge(sems["x_mid"], nth(l, "x_mid", TILES))
                square_sums(l, 2)
                root(l, "norm2", TILES)
                modulate(l, "n2", a2, 3)
                act.wait_ge(*once_full(l, ("router",)))
                b = bank[bank_no(("router",))]
                act.activation(aff[:], b[:, 0:TILES * NE], ACT.Sigmoid).then_inc(bank_read[bank_no(("router",))], 1)
                evac_gates(l, "g2")
                with act.Fori(0, NE) as e:
                    for t in range(TILES):
                        act.wait_ge(*once_full(l, ("G", t), e))
                        b = bank[bank_no(("G", t), e)]
                        act.activation(sg[:, t, :], b[:, :], ACT.Silu).then_inc(bank_read[bank_no(("G", t), e)], 1)
                    for t in range(TILES):
                        act.wait_ge(*once_full(l, ("T", t), e))
                        b = bank[bank_no(("T", t), e)]
                        act.copy(hidT[:, t, :], b[:, :]).then_inc(bank_read[bank_no(("T", t), e)], 1)
            assert count[0] == ACT_STEPS, count[0]

        @block.vector
        def _(dve):
            count = [0]

            def step(l):
                count[0] += 1
                return nth(l, "dve_step", count[0])

            def mean_squares(l, name, n, width):
                k = RMS.index(name) + 1
                dve.tensor_scalar(ms[:, 0:n], ssum[:, 0:n], 1.0 / width, EPS, ALU.mult, ALU.add) \
                    .then_inc(sems["meansq_ready"], 1)
                dve.wait_ge(sems["meansq_ready"], nth(l, "meansq_ready", k))
                dve.wait_ge(sems["rstd_ready"], nth(l, "rstd_ready", k))

            def normalise(l, name, k):
                dve.wait_ge(sems["squares_ready"], nth(l, "squares_ready", k))
                mean_squares(l, name, TILES, D_MODEL)
                for t in range(TILES):
                    dve.tensor_scalar(xn[:, t, :], x[:, t, :], rstd[:, t:t + 1], None, ALU.mult) \
                        .then_inc(sems["normed_tile"], 1)
                    dve.wait_ge(sems["normed_tile"], nth(l, "normed_tile", TILES * (k - 1) + t + 1))

            def modulate(l, what, a, m):
                for c in range(0, KC, 2):
                    dve.wait_ge(*once_full(l, (what, c)))
                    b = bank[bank_no((what, c))]
                    for q, (lo, hi) in enumerate(((0, P), (P, TOK))):
                        ins = dve.tensor_scalar(hT[:, c, lo:hi], b[:, lo:hi], a[:, c, q:q + 1],
                                                modT[:, m, c, q:q + 1], ALU.mult, ALU.add)
                    ins.then_inc(bank_read[bank_no((what, c))], 1)

            def norm_heads(l, p):
                if p < 2:
                    if p == 1:
                        dve.wait_ge(*once_full(l, ("kT", 0, 3)))
                    for t in range(4):
                        src = proj[:, t, O_KR:O_KR + ROPE] if t < 3 else krc[:]
                        dve.tensor_copy(qk[:, 3 + t, :, NOPE:], src.unsqueeze(1).broadcast_to([P, 4, ROPE])) \
                            .then_inc(sems["dve_step"], 1)
                        dve.wait_ge(sems["dve_step"], step(l))
                    dve.wait_ge(*once_read(l, ("q", p, 2)))
                    for lo, hi in ((0, 3), (3, 7)):
                        if lo:
                            dve.wait_ge(*once_read(l, ("kv", p, 3)))
                        m = (hi - lo) * 4
                        dve.tensor_tensor(squares[:, 0:m * QKD], flat(qk[:, lo:hi, :, :]),
                                                 flat(qk[:, lo:hi, :, :]), ALU.mult).then_inc(sems["dve_step"], 1)
                        dve.wait_ge(sems["dve_step"], step(l))
                        dve.tensor_reduce(ssum[:, lo * 4:hi * 4],
                                                 squares[:, 0:m * QKD].rearrange("p (a n) -> p a n", n=QKD), AX, ALU.add) \
                                                     .then_inc(sems["dve_step"], 1)
                        dve.wait_ge(sems["dve_step"], step(l))
                    mean_squares(l, f"heads{p}", 28, QKD)
                    rows_ = qk[:, :, :, :].rearrange("p t h n -> p (t h) n")
                    dve.tensor_tensor(rows_, rows_, last(rstd[:, 0:28], QKD), ALU.mult).then_inc(sems["dve_step"], 1)
                    dve.wait_ge(sems["dve_step"], step(l))
                    d = QKD
                else:
                    dve.wait_ge(*once_read(l, ("proj", 5, 2)))
                    src = proj[:, :, O_NA:O_NA + 512]
                    dve.tensor_tensor(squares[:, :].rearrange("p (t n) -> p t n", t=3), src, src, ALU.mult) \
                        .then_inc(sems["dve_step"], 1)
                    dve.wait_ge(sems["dve_step"], step(l))
                    dve.tensor_reduce(ssum[:, 0:24], squares[:, :].rearrange("p (a n) -> p a n", n=NAD), AX, ALU.add) \
                        .then_inc(sems["dve_step"], 1)
                    dve.wait_ge(sems["dve_step"], step(l))
                    mean_squares(l, "heads2", 24, NAD)
                    dve.wait_ge(*once_full(l, ("kT", 1, 3)))
                    r = rstd[:, 0:24].rearrange("p (t a) -> p t a", t=3)
                    for q in range(2):
                        dve.tensor_tensor(
                            qk[:, 3 * q:3 * q + 3, :, 0:NAD],
                            proj[:, :, O_NA + 256 * q:O_NA + 256 * (q + 1)].rearrange("p t (h n) -> p t h n", h=4),
                            last(r[:, :, 4 * q:4 * q + 4], NAD), ALU.mult).then_inc(sems["dve_step"], 1)
                        dve.wait_ge(sems["dve_step"], step(l))
                    d = NAD
                for lo, hi, at in ((0, 3, R_Q if p < 2 else R_NQ), (3, 7 if p < 2 else 6, R_K if p < 2 else R_NK)):
                    v = qk[:, lo:hi, :, 0:d].rearrange("p t h n -> p (t h) n")
                    g = rowv[:, at:at + d].unsqueeze(1).broadcast_to([P, (hi - lo) * 4, d])
                    ins = dve.scalar_tensor_tensor(v, v, NA_SCALE if (p, lo) == (2, 0) else 1.0, g, ALU.mult, ALU.mult)
                    if p < 2 or lo == 0:
                        ins.then_inc(sems["dve_step"], 1)
                        dve.wait_ge(sems["dve_step"], step(l))
                if p < 2:
                    cos, sin = ropes[:, :, 0, :], ropes[:, :, 1, :]
                    m1 = turned[:, 0, :].rearrange("p (t h n) -> p t h n", t=2, h=4)
                    m2 = turned[:, 1, :].rearrange("p (t h n) -> p t h n", t=2, h=4)
                    for lo in (1, 4):
                        v = qk[:, lo:lo + 2, :, NOPE:]
                        dve.tensor_tensor(m1, v, middle(cos, 4), ALU.mult).then_inc(sems["dve_step"], 1)
                        dve.wait_ge(sems["dve_step"], step(l))
                        for a in range(2):
                            dve.tensor_tensor(m2[:, :, :, a::2], v[:, :, :, 1 - a::2], middle(sin[:, :, a::2], 4),
                                                     ALU.mult).then_inc(sems["dve_step"], 1)
                            dve.wait_ge(sems["dve_step"], step(l))
                        ins = dve.tensor_tensor(v, m1, m2, ALU.add)
                        if lo == 1:
                            ins.then_inc(sems["dve_step"], 1)
                            dve.wait_ge(sems["dve_step"], step(l))
                ins.then_inc(sems["heads_normed"], 1)
                dve.wait_ge(sems["heads_normed"], nth(l, "heads_normed", p + 1))

            def flat(ap):
                return ap.rearrange("p t h n -> p (t h n)")

            def maxima(l, g):
                p, h = GROUPS[g]
                for t in range(TILES):
                    dve.wait_ge(*once_full(l, ("S", g, t)))
                    b = bank[bank_no(("S", g, t))]
                    if p == 2 and t:
                        out = biased[:, g % 2, t - 1, :]
                        dve.tensor_copy(out[:, 2 * P:], b[:, 2 * P:TOK]).then_inc(sems["dve_step"], 1)
                        dve.wait_ge(sems["dve_step"], step(l))
                        dve.tensor_tensor(out[:, 0:2 * P], b[:, 0:2 * P], bias[:, t - 1, h, :], ALU.add) \
                            .then_inc(bank_read[bank_no(("S", g, t))], 1)
                        dve.wait_ge(*once_read(l, ("S", g, t)))
                        dve.tensor_reduce(rowmax[:, t:t + 1], out, AX, ALU.max).then_inc(sems["dve_step"], 1)
                        dve.wait_ge(sems["dve_step"], step(l))
                    else:
                        n = P if t == 0 else TOK
                        dve.tensor_reduce(rowmax[:, t:t + 1], b[:, 0:n], AX, ALU.max).then_inc(sems["dve_step"], 1)
                        dve.wait_ge(sems["dve_step"], step(l))
                scale = -MLA_SCALE if p < 2 else -1.0
                dve.tensor_scalar(negmax[:, g, :], rowmax[:], scale, None, ALU.mult).then_inc(sems["negmax_ready"], 1)
                dve.wait_ge(sems["negmax_ready"], nth(l, "negmax_ready", g + 1))

            def outputs(l, g):
                p, h = GROUPS[g]
                dve.reciprocal(rowsum[:, g, :], rowsum[:, g, :]).then_inc(sems["dve_step"], 1)
                dve.wait_ge(sems["dve_step"], step(l))
                dve.wait_ge(*once_full(l, ("O", g)))
                b = bank[bank_no(("O", g))][:, 0:3 * VD].rearrange("p (t n) -> p t n", t=3)
                col = (4 * p + h) * VD
                dve.tensor_tensor(xn[:, :, col:col + VD], b, last(rowsum[:, g, :], VD), ALU.mult) \
                    .then_inc(bank_read[bank_no(("O", g))], 1)

            def router(l):
                e4 = lambda ap: ap.rearrange("p (a k) -> p a k", k=EPG)
                dve.wait_ge(*once_read(l, ("router",)))
                s = e4(sel[:])
                dve.tensor_tensor(sel[:].rearrange("p (t n) -> p t n", t=TILES), aff[:].rearrange("p (t n) -> p t n", t=TILES),
                                         br[:].unsqueeze(1).broadcast_to([P, TILES, NE]), ALU.add) \
                                             .then_inc(sems["dve_step"], 1)
                dve.wait_ge(sems["dve_step"], step(l))
                n = TILES * NG
                hi, lo = rt[:, 0, 0:2 * n].rearrange("p (a k) -> p a k", k=2), rt[:, 1, 0:2 * n].rearrange("p (a k) -> p a k", k=2)
                dve.tensor_tensor(hi, s[:, :, 0::2], s[:, :, 1::2], ALU.max).then_inc(sems["dve_step"], 1)
                dve.wait_ge(sems["dve_step"], step(l))
                dve.tensor_tensor(lo, s[:, :, 0::2], s[:, :, 1::2], ALU.min).then_inc(sems["dve_step"], 1)
                dve.wait_ge(sems["dve_step"], step(l))
                m1, m2, m3 = (last(rt[:, 2, i * n:(i + 1) * n], 1) for i in range(3))
                dve.tensor_tensor(m1, hi[:, :, 0:1], hi[:, :, 1:2], ALU.max).then_inc(sems["dve_step"], 1)
                dve.wait_ge(sems["dve_step"], step(l))
                dve.tensor_tensor(m2, hi[:, :, 0:1], hi[:, :, 1:2], ALU.min).then_inc(sems["dve_step"], 1)
                dve.wait_ge(sems["dve_step"], step(l))
                dve.tensor_tensor(m3, lo[:, :, 0:1], lo[:, :, 1:2], ALU.max).then_inc(sems["dve_step"], 1)
                dve.wait_ge(sems["dve_step"], step(l))
                dve.tensor_tensor(m2, m2, m3, ALU.max).then_inc(sems["dve_step"], 1)
                dve.wait_ge(sems["dve_step"], step(l))
                score = rt[:, 3, 0:n]
                dve.tensor_tensor(last(score, 1), m1, m2, ALU.add).then_inc(sems["dve_step"], 1)
                dve.wait_ge(sems["dve_step"], step(l))
                s3 = score.rearrange("p (t g) -> p t g", g=NG)
                top = rt[:, 3, n:n + TILES]
                dve.tensor_reduce(top, s3, AX, ALU.max).then_inc(sems["dve_step"], 1)
                dve.wait_ge(sems["dve_step"], step(l))
                dve.tensor_tensor(s3, s3, last(top, NG), ALU.is_equal).then_inc(sems["dve_step"], 1)
                dve.wait_ge(sems["dve_step"], step(l))
                dve.tensor_tensor(s3, s3, tiew[:].unsqueeze(1).broadcast_to([P, TILES, NG]), ALU.mult) \
                    .then_inc(sems["dve_step"], 1)
                dve.wait_ge(sems["dve_step"], step(l))
                dve.tensor_reduce(top, s3, AX, ALU.max).then_inc(sems["dve_step"], 1)
                dve.wait_ge(sems["dve_step"], step(l))
                dve.tensor_tensor(s3, s3, last(top, NG), ALU.is_equal).then_inc(sems["dve_step"], 1)
                dve.wait_ge(sems["dve_step"], step(l))
                rank, cmp = e4(rt[:, 4, :]), e4(rt[:, 5, :])
                dve.memset(rt[:, 4, :], 0.0).then_inc(sems["dve_step"], 1)
                dve.wait_ge(sems["dve_step"], step(l))
                for j in range(EPG):
                    sj = s[:, :, j:j + 1]
                    if j:
                        dve.tensor_tensor(cmp[:, :, 0:j], sj.broadcast_to([P, n, j]), s[:, :, 0:j], ALU.is_gt) \
                            .then_inc(sems["dve_step"], 1)
                        dve.wait_ge(sems["dve_step"], step(l))
                        dve.tensor_tensor(rank[:, :, 0:j], rank[:, :, 0:j], cmp[:, :, 0:j], ALU.add) \
                            .then_inc(sems["dve_step"], 1)
                        dve.wait_ge(sems["dve_step"], step(l))
                    if j < EPG - 1:
                        k = EPG - 1 - j
                        dve.tensor_tensor(cmp[:, :, j + 1:], sj.broadcast_to([P, n, k]), s[:, :, j + 1:], ALU.is_ge) \
                            .then_inc(sems["dve_step"], 1)
                        dve.wait_ge(sems["dve_step"], step(l))
                        dve.tensor_tensor(rank[:, :, j + 1:], rank[:, :, j + 1:], cmp[:, :, j + 1:], ALU.add) \
                            .then_inc(sems["dve_step"], 1)
                        dve.wait_ge(sems["dve_step"], step(l))
                dve.tensor_scalar(rt[:, 4, :], rt[:, 4, :], float(TOP_K), None, ALU.is_lt) \
                    .then_inc(sems["dve_step"], 1)
                dve.wait_ge(sems["dve_step"], step(l))
                dve.tensor_tensor(rank, rank, last(score, EPG), ALU.mult).then_inc(sems["dve_step"], 1)
                dve.wait_ge(sems["dve_step"], step(l))
                dve.tensor_tensor(rt[:, 4, :], rt[:, 4, :], aff[:], ALU.mult).then_inc(sems["dve_step"], 1)
                dve.wait_ge(sems["dve_step"], step(l))
                w = rt[:, 4, :].rearrange("p (t n) -> p t n", t=TILES)
                dve.tensor_reduce(top, w, AX, ALU.add).then_inc(sems["dve_step"], 1)
                dve.wait_ge(sems["dve_step"], step(l))
                dve.reciprocal(top, top).then_inc(sems["dve_step"], 1)
                dve.wait_ge(sems["dve_step"], step(l))
                dve.tensor_tensor(gates[:], w, last(top, NE), ALU.mult).then_inc(sems["dve_step"], 1)
                dve.wait_ge(sems["dve_step"], step(l))

            dve.wait_ge(consts_loaded, N_CONST)
            dve.wait_ge(consts_made, 1 + NG)
            dve.wait_ge(cond_exp, 1)
            dve.tensor_scalar(cond_e[:], cond_e[:], 1.0, None, ALU.add).then_inc(cond_exp, 1)
            dve.wait_ge(cond_exp, 2)
            dve.reciprocal(cond_e[:], cond_e[:]).then_inc(cond_exp, 1)
            dve.wait_ge(cond_exp, 3)
            dve.tensor_tensor(condT[:], condT[:], cond_e[:], ALU.mult).then_inc(cond_ready, 1)
            with dve.Fori(0, DEPTH) as l:
                count[0] = 0
                normalise(l, "norm1", 1)
                dve.wait_ge(sems["small_loaded"], nth(l, "small_loaded", PER_LAYER["small_loaded"]))
                for m in range(6):
                    dve.wait_ge(*once_full(l, ("mod", m)))
                    b = bank[bank_no(("mod", m))]
                    ada_b = vecs[:, V_ADA + m * KC:V_ADA + (m + 1) * KC]
                    dve.tensor_tensor(modT[:, m, :, :], b[:, 0:2 * KC].rearrange("p (c q) -> p c q", q=2),
                                            last(ada_b, 2), ALU.add).then_inc(bank_read[bank_no(("mod", m))], 1)
                    dve.wait_ge(*once_read(l, ("mod", m)))
                for k, (a, at, m) in enumerate(((a1, V_N1, 1), (a2, V_N2, 4))):
                    dve.scalar_tensor_tensor(a[:], modT[:, m, :, :], 1.0, last(vecs[:, at:at + KC], 2),
                                                     ALU.add, ALU.mult).then_inc(sems["mod_ready"], 1)
                    dve.wait_ge(sems["mod_ready"], nth(l, "mod_ready", k + 1))
                modulate(l, "n1", a1, 0)
                dve.wait_ge(sems["bias_loaded"], nth(l, "bias_loaded", PER_LAYER["bias_loaded"]))
                bias_rows = bias[:, :, :, :].rearrange("p t h (j k) -> p (t h j) k", k=GRID_W)
                dve.tensor_tensor(bias_rows, bias_rows, mask[:].unsqueeze(1).broadcast_to([P, 32, GRID_W]), ALU.add) \
                    .then_inc(sems["dve_step"], 1)
                dve.wait_ge(sems["dve_step"], step(l))
                for q, (at, n) in enumerate(((0, QL), (O_KV, KVL))):
                    for t in range(TILES):
                        dve.wait_ge(*once_read(l, ("proj", q, t)))
                        src = proj[:, t, at:at + n]
                        dve.tensor_tensor_reduce(squares[:, 0:n], src, src, 1.0, 0.0, ALU.mult, ALU.add,
                                                        ssum[:, 3 * q + t:3 * q + t + 1]) \
                                                            .then_inc(sems["dve_step"], 1)
                        dve.wait_ge(sems["dve_step"], step(l))
                dve.tensor_scalar(ssum[:, 3:6], ssum[:, 3:6], QL / KVL, None, ALU.mult).then_inc(sems["dve_step"], 1)
                dve.wait_ge(sems["dve_step"], step(l))
                mean_squares(l, "latent", 6, QL)
                for t in range(TILES):
                    dve.tensor_scalar(q_lat_n[:, t, :], proj[:, t, 0:QL], rstd[:, t:t + 1], None, ALU.mult) \
                        .then_inc(sems["dve_step"], 1)
                    dve.wait_ge(sems["dve_step"], step(l))
                for t in range(TILES):
                    ins = dve.scalar_tensor_tensor(ckvn[:, t, :], proj[:, t, O_KV:O_KV + KVL], rstd[:, 3 + t:4 + t],
                                                   rowv[:, R_KV:R_KV + KVL], ALU.mult, ALU.mult)
                ins.then_inc(sems["latents_normed"], 1)
                dve.wait_ge(sems["latents_normed"], nth(l, "latents_normed", 1))
                for c in range(2):
                    dve.wait_ge(*once_full(l, ("ql", c)))
                    b = bank[bank_no(("ql", c))]
                    dve.tensor_scalar(qlatT[:, c, :], b[:, 0:TOK], vecs[:, V_QAG + c:V_QAG + c + 1], None, ALU.mult) \
                        .then_inc(bank_read[bank_no(("ql", c))], 1)
                dve.wait_ge(*once_full(l, ("ckv",)))
                b = bank[bank_no(("ckv",))]
                dve.tensor_copy(ckvT[:, 0:TOK], b[:, 0:TOK]).then_inc(bank_read[bank_no(("ckv",))], 1)
                dve.wait_ge(sems["gate_sigmoid"], nth(l, "gate_sigmoid", 1))
                dve.tensor_tensor(glu, proj[:, :, O_A:O_A + CONV_CH], proj[:, :, O_G:O_G + CONV_CH], ALU.mult) \
                    .then_inc(sems["glu_ready"], 1)
                dve.wait_ge(sems["glu_ready"], nth(l, "glu_ready", 1))
                for c in range(2):
                    dve.wait_ge(*once_full(l, ("conv", c)))
                    b = bank[bank_no(("conv", c))]
                    dve.tensor_copy(conv_in[:, c, C_CTX:C_CTX + P], b[:, 0:P]).then_inc(sems["dve_step"], 1)
                    dve.wait_ge(sems["dve_step"], step(l))
                    dve.tensor_copy(conv_in[:, c, C_LAT:C_LAT + 2 * P], b[:, P:TOK]) \
                        .then_inc(bank_read[bank_no(("conv", c))], 1)
                norm_heads(l, 0)
                norm_heads(l, 1)
                for c in range(2):
                    tap = lambda k: vecs[:, V_TAP + 2 * k + c:V_TAP + 2 * k + c + 1]
                    dve.tensor_scalar(conv_acc[:, c, :], conv_in[:, c, 0:C_OUT], tap(0),
                                             vecs[:, V_DWB + c:V_DWB + c + 1], ALU.mult, ALU.add) \
                                                 .then_inc(sems["dve_step"], 1)
                    dve.wait_ge(sems["dve_step"], step(l))
                    for k in range(1, TAPS):
                        ins = dve.scalar_tensor_tensor(conv_acc[:, c, :], conv_in[:, c, k:k + C_OUT], tap(k),
                                                       conv_acc[:, c, :], ALU.mult, ALU.add)
                        if (c, k) != (1, TAPS - 1):
                            ins.then_inc(sems["dve_step"], 1)
                            dve.wait_ge(sems["dve_step"], step(l))
                ins.then_inc(sems["conv_done"], 1)
                dve.wait_ge(sems["conv_done"], nth(l, "conv_done", 1))
                for i in range(len(GROUPS) + 2):
                    if i < len(GROUPS):
                        maxima(l, i)
                    if 1 <= i <= len(GROUPS):
                        dve.wait_ge(*once_full(l, ("PT", i - 1, 0)))
                        b = bank[bank_no(("PT", i - 1, 0))]
                        dve.tensor_copy(probsT[:, (i - 1) % 2, 0:4 * P], b[:, :]) \
                            .then_inc(bank_read[bank_no(("PT", i - 1, 0))], 1)
                    if i >= 2:
                        outputs(l, i - 2)
                    if i == 3:
                        norm_heads(l, 2)
                    if i == 9:
                        for t in range(TILES):
                            dve.wait_ge(*once_full(l, ("cb", t)))
                            b = bank[bank_no(("cb", t))]
                            dve.bn_stats(stats[:, t, :], b[:, 0:CONV_CH]).then_inc(sems["dve_step"], 1)
                            dve.wait_ge(sems["dve_step"], step(l))
                            dve.sem_inc(carried, 1)
                            dve.bn_aggr(meanvar[:, t, :], stats[:, t, :]).then_inc(sems["dve_step"], 1)
                            dve.wait_ge(sems["dve_step"], step(l))
                        dve.tensor_copy(ssum[:, 0:TILES], meanvar[:, :, 1]).then_inc(sems["dve_step"], 1)
                        dve.wait_ge(sems["dve_step"], step(l))
                        mean_squares(l, "conv", TILES, 1)
                        for t in range(TILES):
                            dve.wait_ge(*once_full(l, ("cb", t)))
                            b = bank[bank_no(("cb", t))]
                            dve.tensor_scalar(ln_tm[:, t, :], b[:, 0:CONV_CH], meanvar[:, t, 0:1], rstd[:, t:t + 1],
                                                    ALU.subtract, ALU.mult).then_inc(bank_read[bank_no(("cb", t))], 1)
                    if i == 10:
                        for c in range(2):
                            dve.wait_ge(*once_full(l, ("ln", c)))
                            b = bank[bank_no(("ln", c))]
                            dve.tensor_scalar(z_conv[:, c, :], b[:, 0:TOK], vecs[:, V_LNG + c:V_LNG + c + 1],
                                                    vecs[:, V_LNB + c:V_LNB + c + 1], ALU.mult, ALU.add) \
                                                        .then_inc(bank_read[bank_no(("ln", c))], 1)
                            dve.wait_ge(*once_read(l, ("ln", c)))
                dve.wait_ge(*once_read(l, ("g1", 1, 1)))
                for j in range(OUT_SLOTS):
                    for t in range(TILES):
                        dve.wait_ge(*once_full(l, ("out", j, t)))
                        b = bank[bank_no(("out", j, t))]
                        cols = slice(j * 256, (j + 1) * 256)
                        dve.tensor_tensor(gated[:, 0:256], b[:, 0:256], G[:, min(t, 1), cols], ALU.mult) \
                            .then_inc(bank_read[bank_no(("out", j, t))], 1)
                        dve.wait_ge(*once_read(l, ("out", j, t)))
                        ins = dve.tensor_tensor(x[:, t, cols], x[:, t, cols], gated[:, 0:256], ALU.add)
                        if j == OUT_SLOTS - 1:
                            ins.then_inc(sems["x_mid"], 1)
                            dve.wait_ge(sems["x_mid"], nth(l, "x_mid", t + 1))
                        else:
                            ins.then_inc(sems["dve_step"], 1)
                            dve.wait_ge(sems["dve_step"], step(l))
                normalise(l, "norm2", 2)
                modulate(l, "n2", a2, 3)
                router(l)
                dve.memset(acc, 0.0).then_inc(sems["dve_step"], 1)
                dve.wait_ge(sems["dve_step"], step(l))
                dve.sem_inc(carried, 1)
                with dve.Fori(0, NE) as e:
                    for t in range(TILES):
                        dve.wait_ge(*once_full(l, ("U", t), e))
                        b = bank[bank_no(("U", t), e)]
                        dve.wait_ge(*once_read(l, ("G", t), e))
                        dve.scalar_tensor_tensor(hid[:, t, :], b[:, :], gates[:, t, bass.ds(e, 1)], sg[:, t, :],
                                                       ALU.mult, ALU.mult) \
                                                           .then_inc(bank_read[bank_no(("U", t), e)], 1)
                    for t in range(TILES):
                        for n in range(2):
                            dve.wait_ge(*once_full(l, ("Y", t, n), e))
                            b = bank[bank_no(("Y", t, n), e)]
                            part = acc[:, t, n * 512:(n + 1) * 512]
                            dve.tensor_tensor(part, part, b[:, :], ALU.add) \
                                .then_inc(bank_read[bank_no(("Y", t, n), e)], 1)
                            dve.wait_ge(*once_read(l, ("Y", t, n), e))
                dve.wait_ge(*once_read(l, ("g2", 1, 1)))
                for t in range(TILES):
                    dve.tensor_tensor(acc[:, t, :], acc[:, t, :], G[:, min(t, 1), :], ALU.mult) \
                        .then_inc(sems["dve_step"], 1)
                    dve.wait_ge(sems["dve_step"], step(l))
                    ins = dve.tensor_tensor(x[:, t, :], x[:, t, :], acc[:, t, :], ALU.add)
                    if t < TILES - 1:
                        ins.then_inc(sems["dve_step"], 1)
                        dve.wait_ge(sems["dve_step"], step(l))
                ins.then_inc(sems["x_done"], 1)
            assert count[0] == DVE_STEPS, count[0]


def _layout(i):
    f = {k: np.ascontiguousarray(v) for k, v in i.items()}
    L = DEPTH
    wring = np.zeros((L, LAYER_SLOTS, P, SLOT), np.float32)

    def by_columns(w, n):
        return w.reshape(L, KC, P, -1, n).transpose(0, 3, 2, 1, 4).reshape(L, -1, P, KC * n)

    wring[:, 0:S_IN] = by_columns(f["w_ada"], 256)
    full = 256 * (IN_SLOTS - 1)
    wring[:, S_IN:S_UP - 1] = by_columns(f["w_in"][:, :, :full], 256)
    wring[:, S_UP - 1, :, :KC * LAST_W] = by_columns(f["w_in"][:, :, full:], LAST_W)[:, 0]
    wring[:, S_UP - 1, :, KC * LAST_W:KC * LAST_W + 512] = f["w_kv_up"][:, :, 512:]
    wring[:, S_UP, :, :1536] = f["w_q_up"].reshape(L, 2, P, 768).transpose(0, 2, 1, 3).reshape(L, P, 1536)
    wring[:, S_UP, :, 1536:] = f["w_kv_up"][:, :, :512]
    wring[:, S_OUT:S_EXP] = by_columns(f["w_out"], 256)
    ex = wring[:, S_EXP:].reshape(L, NE, PER_EXPERT, P, SLOT)
    for s, name, k in ((0, "w_e_gate", 4), (2, "w_e_up", 4), (4, "w_e_down", 2)):
        w = f[name]
        ex[:, :, s:s + 2] = w.reshape(L, NE, 2, k, P, -1).transpose(0, 1, 2, 4, 3, 5).reshape(L, NE, 2, P, SLOT)

    def columns(v):
        return v.reshape(L, -1, P).transpose(0, 2, 1)

    vec = np.concatenate([columns(f[n]) for n in ("b_ada", "norm1_g", "norm2_g", "conv_dw_b", "conv_ln_g",
                                                  "conv_ln_b", "q_a_g")] + [columns(f["conv_dw_w"].reshape(L, -1))], 2)
    rows = np.concatenate([f[n] for n in ("mla_q_norm_g", "mla_k_norm_g", "na_q_norm_g", "na_k_norm_g", "kv_a_g")], 1)
    rpb = f["na_rpb"]
    far = GRID_W - WIN_W
    padded = np.pad(rpb, ((0, 0), (0, 0), (0, 0), (far, far)))
    at = GRID_W - 1 + np.arange(GRID_W)[None, :] - np.arange(GRID_W)[:, None]
    na_bias = padded[:, :, :, at].transpose(0, 3, 1, 2, 4)
    tok = np.arange(2 * P)
    inv = (10000.0 ** (-np.arange(ROPE // 4, dtype=np.float32) / (ROPE // 4))).astype(np.float32)
    ang = np.concatenate([(tok // GRID_W).astype(np.float32)[:, None] * inv,
                          (tok % GRID_W).astype(np.float32)[:, None] * inv], 1)
    cos, sin = np.cos(ang), np.sin(ang)
    table = np.stack([np.repeat(cos, 2, 1), np.stack([-sin, sin], 2).reshape(2 * P, ROPE)], 1)
    rope = table.reshape(2, P, 2, ROPE).transpose(1, 0, 2, 3)
    q = np.arange(P) % GRID_W
    c0 = np.clip(q - WIN_W // 2, 0, GRID_W - WIN_W)
    k = np.arange(GRID_W)
    mask = np.where((k[None] >= c0[:, None]) & (k[None] < c0[:, None] + WIN_W), 0.0, MASKED)
    x = np.concatenate([f["x_prompt"][0], f["x_sample"][0]], 0).reshape(TILES, P, D_MODEL).transpose(1, 0, 2)
    cond = np.stack([f["c_ctx"].reshape(KC, P).T, f["c"][0].reshape(KC, P).T], 2)
    out = dict(
        wring=wring.reshape(L * LAYER_SLOTS, P, SLOT), x_in=x, vec=vec, rows=rows,
        ckv_cache=f["cache_mla_ckv"][0].transpose(0, 2, 1), kr_cache=f["cache_mla_krope"][0],
        nak_cache=f["cache_na_k"][0].transpose(0, 3, 2, 1), nav_cache=f["cache_na_v"][0], cond=cond,
        w_router=f["w_router"].reshape(KC, P, NE).transpose(1, 0, 2), b_router=f["b_router"],
        rope=rope, ident=np.eye(P), na_mask=mask, na_bias=na_bias)
    return {n: np.ascontiguousarray(a, dtype=np.float32) for n, a in out.items()}


OUTS = dict(y_prompt=(P, D_MODEL), y_sample=(2 * P, D_MODEL), new_ckv=(DEPTH, P, KVL), new_krope=(DEPTH, P, ROPE),
            new_nak=(DEPTH, P, NAH * NAD), new_nav=(DEPTH, P, NAH * NAD))


def program(nc, arrays):
    args = {n: nc.dram_tensor(n + "_dram", a.shape, F32, kind="ExternalInput").ap() for n, a in arrays.items()}
    outs = {n: nc.dram_tensor(n + "_dram", s, F32, kind="ExternalOutput").ap() for n, s in OUTS.items()}
    build(nc, **args, **outs)


def kernel(**inputs):
    import concourse.bacc as bacc
    from concourse.bass_utils import run_bass_kernel_spmd

    nc = bacc.Bacc("TRN2", target_bir_lowering=False, num_devices=1)
    arrays = _layout({k: np.asarray(v) for k, v in inputs.items()})
    program(nc, arrays)
    r = run_bass_kernel_spmd(nc, [{n + "_dram": a for n, a in arrays.items()}], core_ids=[0])
    got = {n: r.results[0][n + "_dram"] for n in OUTS}
    return (got["y_prompt"].reshape(1, P, D_MODEL), got["y_sample"].reshape(1, 2 * P, D_MODEL),
            got["new_ckv"].reshape(1, DEPTH, P, KVL), got["new_krope"].reshape(1, DEPTH, P, ROPE),
            got["new_nak"].reshape(1, DEPTH, P, NAH, NAD), got["new_nav"].reshape(1, DEPTH, P, NAH, NAD))
```

```python
from collections import namedtuple
from contextlib import ExitStack

import concourse.bass as bass
import numpy as np
from concourse import mybir

F32, I32 = mybir.dt.float32, mybir.dt.int32
F32R = mybir.dt.float32r
ALU = mybir.AluOpType
ACT = mybir.ActivationFunctionType
AX = mybir.AxisListType.X

P = 128
D_MODEL, DEPTH, GRID_W = 1024, 2, 64
KC = D_MODEL // P
TILES = 3
TOK = TILES * P
HEADS, NOPE, ROPE, VD = 8, 64, 32, 64
QKD = NOPE + ROPE
QL, KVL = 256, 128
CONV_CH, TAPS = 256, 31
NAH, NAD = 4, 64
NE, NG, EPG, TOP_K, FF = 16, 4, 4, 2, 512
FC = FF // P
CAP = 128
PASSES = -(-TOK // CAP)
EPS = 1e-6
MLA_SCALE, NA_SCALE = QKD ** -0.5, NAD ** -0.5
WIN_H, WIN_W = 8, 16
MASKED = -1e30
IN_COLS = QL + KVL + ROPE + 2 * CONV_CH + 3 * NAH * NAD
O_KV, O_KR, O_A, O_G = QL, QL + KVL, QL + KVL + ROPE, QL + KVL + ROPE + CONV_CH
O_NA = O_G + CONV_CH

RING, SLOT = 6, 2048
ADA_SLOTS = 6 * D_MODEL // 256
IN_SLOTS = -(-IN_COLS // 256)
OUT_SLOTS = D_MODEL // 256
S_IN = ADA_SLOTS
S_UP = S_IN + IN_SLOTS
S_OUT = S_UP + 1
S_EXP = S_OUT + OUT_SLOTS
PER_EXPERT = 6
SPLIT = 4
LAYER_SLOTS = S_EXP + NE * PER_EXPERT
LAST_W = IN_COLS - 256 * (IN_SLOTS - 1)
assert S_EXP % RING == 0 and LAYER_SLOTS % RING == 0 and RING == PER_EXPERT

V_ADA, V_N1, V_N2, V_DWB, V_LNG, V_LNB, V_QAG, V_TAP = 0, 48, 56, 64, 66, 68, 70, 72
DVE_STEPS = 190 + PASSES
VEC = V_TAP + 2 * TAPS
R_Q, R_K, R_NQ, R_NK, R_KV = 0, QKD, 2 * QKD, 2 * QKD + NAD, 2 * QKD + 2 * NAD
ROWS = R_KV + KVL

PAD = TAPS // 2
C_CTX, C_LAT = PAD, 2 * PAD + P
C_LEN = 3 * PAD + TOK
C_OUT = C_LEN - 2 * PAD

RMS = ["norm1", "latent", "heads0", "heads1", "heads2", "conv", "norm2"]
ROOT_AT = 13
GROUPS = [(p, h) for p in range(3) for h in range(4)]

PER_LAYER = dict(
    small_loaded=16 * 5, bias_loaded=16 * 16, na_cache_loaded=16, mod_ready=2, squares_ready=2,
    meansq_ready=len(RMS), rstd_ready=len(RMS), normed_tile=2 * TILES, latents_normed=1,
    gate_sigmoid=1, glu_ready=1, conv_steps=2 * TAPS, conv_lower=1, conv_mixed=1,
    heads_normed=3, negmax_ready=len(GROUPS), na_exp_done=2 * 4, x_mid=TILES, x_done=1,
    latents_stored=16, values_stored=16 * 2, keys_stored=16, chosen=1, acc_cleared=1, h_hi_made=2 * TILES, dve_step=DVE_STEPS,
)


def heads_transposed(p):
    return [(kind, p, h) for h in range(4) for kind in ("qT", "kT")]


def psum_plan():
    order = []
    for s in range(ADA_SLOTS):
        order += [("ada", s)]
        if s % 4 == 0 and s:
            order += [("mod", s // 4 - 1)]
    order += [("mod", 5)] + [("n1", c) for c in range(KC)]
    order += [("proj", j, t) for j in range(4) for t in range(TILES)]
    order += [("ql", 0), ("ql", 1), ("ckv",)]
    order += [("proj", 4, t) for t in range(TILES)]
    order += [("conv", 0), ("conv", 1)]
    order += [("q", 0, t) for t in range(3)] + [("kv", 0, t) for t in range(4)]
    order += [("proj", j, t) for j in (5, 6) for t in range(TILES)]
    order += heads_transposed(0)
    order += [("q", 1, t) for t in range(3)] + [("kv", 1, t) for t in range(4)]
    for i in range(len(GROUPS) + 2):
        if i < len(GROUPS):
            order += [("S", i, t) for t in range(3)]
        if 1 <= i <= len(GROUPS):
            order += [("PT", i - 1, 0), ("PT", i - 1, 1)]
        if i >= 2:
            order += [("O", i - 2)]
        if i == 3:
            order += heads_transposed(1)
        if i == 7:
            order += heads_transposed(2)
        if i == 9:
            order += [("cb", t) for t in range(3)]
        if i == 10:
            order += [("ln", 0), ("ln", 1)]
    order += [("g1", c, n) for c in range(2) for n in range(2)]
    order += [("mix", c) for c in range(6)]
    order += [("out", j, t) for j in range(OUT_SLOTS) for t in range(3)]
    order += [("n2", c) for c in range(KC)] + [("router",)]
    order += [("h", t, n) for t in range(TILES) for n in range(2)] + [("place",)]
    order += [("g2", c, n) for c in range(2) for n in range(2)]
    return {name: n for n, name in enumerate(order)}


PLAN = psum_plan()
BANKS = 8
SPARE = -len(PLAN) % BANKS
LEAD = (len(PLAN) + SPARE) // BANKS

SCAT = 2 * TILES
PER_E = 2
EXPERT = {("gather", k): k - 6 for k in range(4)}
EXPERT.update({("ST",): -2, ("G",): -1, ("U",): 0, ("T",): 1 + SCAT // 2, ("Y", 0): 8, ("Y", 1): 9})
EXPERT.update({("scatter", k): 17 + k + (k >= SCAT // 2) for k in range(SCAT)})
FIRST = {("gather", k): k for k in range(4)}
FIRST.update({("ST",): 4, ("G",): 5, ("U",): 6, ("T",): 7})
LAST = {("scatter", k): 10 + k for k in range(SCAT)}
assert PER_E * BANKS == 4 + 1 + 1 + 1 + 1 + 2 + SCAT

Layer = namedtuple("Layer", "n passes turns loads")
Visit = namedtuple("Visit", "layer pass_no pair k")


def build(nc, wring, x_in, vec, rows, ckv_cache, kr_cache, nak_cache, nav_cache, cond, w_router,
          b_router, rope, shape_consts, na_mask, na_bias,
          y_prompt, y_sample, new_ckv, new_krope, new_nak, new_nav):
    with ExitStack() as ctx:
        def sb(name, *shape):
            return ctx.enter_context(nc.sbuf_tensor(name, list(shape), F32))

        def overlay(name, dtype, *shape):
            size = 4 * int(np.prod(shape[1:]))
            t = nc.alloc_sbuf_tensor_at(name, list(shape), dtype, offset=lent[0])
            lent[0] += size
            assert lent[0] <= lent[1]
            return t

        def sem(name):
            return ctx.enter_context(nc.semaphore(name))

        ring = sb("ring", P, RING, SLOT)
        x = sb("x", P, TILES, D_MODEL)
        lent = [-(-nc.sbuf_base // 32) * 32]
        hT = sb("hT", P, KC, TOK)
        xn = sb("xn", P, TILES, D_MODEL)
        proj = sb("proj", P, TILES, IN_COLS)
        v_mla = sb("v_mla", P, 4, HEADS, VD)
        qT = sb("qT", P, 2, 4, TOK)
        qk = sb("qk", P, 7, 4, QKD)
        squares = sb("squares", P, 1536)
        probs = sb("probs", P, 2, 7 * P)
        probsT = sb("probsT", P, 2, 7 * P)
        biased = sb("biased", P, 2, 2, TOK)
        bias = sb("bias", P, 2, NAH, 2 * P)
        conv_acc = sb("conv_acc", P, 2, C_OUT)
        qlatT = sb("qlatT", P, 2, TOK)
        ckvT = sb("ckvT", P, TOK + P)
        ckvn = sb("ckvn", P, TILES, KVL)
        krc = sb("krc", P, ROPE)
        nav = sb("nav", P, NAH, NAD)
        lent.append(-(-nc.sbuf_base // 32) * 32 + 4 * 4 * (TOK + P))
        kT = sb("kT", P, 2, 4, TOK + P)
        conv_in = sb("conv_in", P, 2, C_LEN)
        modT = sb("modT", P, 6, KC, 2)
        a1 = sb("a1", P, KC, 2)
        a2 = sb("a2", P, KC, 2)
        vecs = sb("vecs", P, VEC)
        rowv = sb("rowv", P, ROWS)
        condT = sb("condT", P, KC, 2)
        cond_e = sb("cond_e", P, KC, 2)
        wr = sb("wr", P, KC, NE)
        br = sb("br", P, NE)
        ropes = sb("ropes", P, 2, 2, ROPE)
        shapes = sb("shapes", P, 3, P)
        iden = shapes[:, 0, :]
        ones = sb("ones", P, 1)
        scratch = sb("scratch", P, 6 * TILES * NE)
        chosen = sb("chosen", P, TILES * NE)
        place = sb("place", P, TILES * NE)
        crowd = sb("crowd", P, 2)
        tally = sb("tally", 1, 3)
        growth = sb("growth", 1, 3)
        tally_i = ctx.enter_context(nc.sbuf_tensor("tally_i", [1, 3], I32))
        mask = sb("mask", P, GRID_W)
        ssum = sb("ssum", P, 32)
        ms = sb("ms", P, 32)
        half = sb("half", P, 1)
        rstd = sb("rstd", P, 32)
        stats = sb("stats", P, TILES, 6)
        meanvar = sb("meanvar", P, TILES, 2)
        negmax = sb("negmax", P, 12, 3)
        rowmax = sb("rowmax", P, 3)
        rowsum = sb("rowsum", P, 12, 3)
        aff = sb("aff", P, TILES * NE)
        sel = sb("sel", P, TILES * NE)
        gates = sb("gates", P, TILES, NE)
        tiew = sb("tiew", P, NG)
        bank = [ctx.enter_context(nc.psum_tensor(f"bank{i}", [P, 512], F32)) for i in range(BANKS)]

        modrow = qT[0:2, :, :, :].rearrange("p a h n -> p (a h n)")[:, 0:2048].rearrange("p (b n) -> p b n", b=2)
        G = kT[:, 1, :, :].rearrange("p h n -> p (h n)").rearrange("p (c n) -> p c n", c=2)
        tap_product = biased[:, :, :, :].rearrange("p a b n -> p (a b n)")[:, 0:C_OUT]
        turned = squares[:, 0:4 * 4 * ROPE].rearrange("p (a n) -> p a n", a=2)
        q_lat_n = probsT[:, 0, 0:TILES * QL].rearrange("p (t n) -> p t n", t=TILES)
        glu = probs[:, 0, 0:TILES * CONV_CH].rearrange("p (t n) -> p t n", t=TILES)
        ln_tm = squares[:, 0:TILES * CONV_CH].rearrange("p (t n) -> p t n", t=TILES)
        z_conv = squares[:, CONV_CH * TILES:2 * CONV_CH * TILES].rearrange("p (c n) -> p c n", c=2)
        rt = scratch[:].rearrange("p (a n) -> p a n", a=6)

        y_hi, y_lo = (overlay(n, F32R, P, D_MODEL) for n in ("y_hi", "y_lo"))
        hidT_hi, hidT_lo = (overlay(n, F32R, P, FC, P) for n in ("hidT_hi", "hidT_lo"))
        h_hi, h_lo = (overlay(n, F32R, P, TILES, D_MODEL) for n in ("h_hi", "h_lo"))
        hg_hi, hg_lo = (overlay(n, F32R, P, KC, P) for n in ("hg_hi", "hg_lo"))
        pick = overlay("pick", F32R, P, TILES, P)
        pickT = overlay("pickT", F32R, P, 2, TILES * P)
        w_hi, w_lo = (overlay(n, F32R, P, SPLIT, SLOT) for n in ("w_hi", "w_lo"))
        acc = overlay("acc", F32, P, TILES, D_MODEL)
        sg = overlay("sg", F32, P, FF)
        iden_r = overlay("iden_r", F32R, P, P)

        sems = {name: sem(name) for name in PER_LAYER}
        consts_loaded, consts_made = sem("consts_loaded"), sem("consts_made")
        cond_exp, cond_ready = sem("cond_exp"), sem("cond_ready")
        carried = sem("carried")
        slot_full = [sem(f"slot_full{i}") for i in range(RING)]
        slot_free = [sem(f"slot_free{i}") for i in range(RING)]
        bank_full = [sem(f"bank_full{i}") for i in range(BANKS)]
        bank_read = [sem(f"bank_read{i}") for i in range(BANKS)]
        outputs_stored = sem("outputs_stored")
        passes_counted = sem("passes_counted")
        placed = sem("placed")
        pick_made, hidT_hi_made, y_hi_made = sem("pick_made"), sem("hidT_hi_made"), sem("y_hi_made")
        hi_made = [sem(f"hi_made{i}") for i in range(SPLIT)]
        lo_made = [sem(f"lo_made{i}") for i in range(SPLIT)]
        split_used = [sem(f"split_used{i}") for i in range(SPLIT)]
        N_CONST = 16 * 7

        def nth(l, name, k):
            return l.n * PER_LAYER[name] + k

        def turn_of(v, key):
            if v.pair is None:
                return (FIRST if v.k == 0 else LAST if v.k == NE - 1 else EXPERT).get(key, EXPERT[key])
            return EXPERT[key]

        def bank_no(at, key):
            return (PLAN[key] if isinstance(at, Layer) else turn_of(at, key)) % BANKS

        def turns_before(at, key, more):
            if isinstance(at, Layer):
                return at.turns + (PLAN[key] // BANKS + more)
            first = LEAD + PER_E * at.k + turn_of(at, key) // BANKS + more
            if at.pair is None:
                return at.layer.n * LEAD + (at.pass_no * (PER_E * NE) + first)
            return at.layer.n * LEAD + (at.pass_no * (PER_E * NE) + (at.pair * (2 * PER_E) + first))

        def once_free(at, key):
            return bank_read[bank_no(at, key)], turns_before(at, key, 1)

        def once_full(at, key):
            return bank_full[bank_no(at, key)], turns_before(at, key, 1)

        def once_read(at, key):
            return bank_read[bank_no(at, key)], turns_before(at, key, 2)

        def once_loaded(l, s):
            return slot_full[s % RING], l.loads + 16 * (s // RING + 1)

        def visits(v, per_visit, more):
            first = per_visit * v.k + more
            if v.pair is None:
                return v.pass_no * (per_visit * NE) + first
            return v.pass_no * (per_visit * NE) + (v.pair * (2 * per_visit) + first)

        def expert_loaded(v, i):
            return slot_full[i], v.layer.n * (16 * S_EXP // RING) + visits(v, 16, 16 * (S_EXP // RING + 1))

        def split_no(v, i):
            return (PER_EXPERT * v.k + i) % SPLIT

        def uses_before(v, i, more):
            first = (PER_EXPERT * v.k + i) // SPLIT + more
            if v.pair is None:
                return v.pass_no * (PER_EXPERT * NE // SPLIT) + first
            return v.pass_no * (PER_EXPERT * NE // SPLIT) + (v.pair * (2 * PER_EXPERT // SPLIT) + first)

        def once_split_free(v, i):
            return split_used[split_no(v, i)], uses_before(v, i, 1)

        def once_hi(v, i):
            return hi_made[split_no(v, i)], uses_before(v, i, 3)

        def once_split(v, i):
            return lo_made[split_no(v, i)], uses_before(v, i, 3)

        def before(v):
            return v._replace(k=v.k - 1)

        def after(v):
            return v._replace(k=v.k + 1)

        def layer_at(engine, n):
            return Layer(n, *[engine.value_load(tally_i[0:1, i:i + 1], min_val=0, max_val=most)
                              for i, most in enumerate((DEPTH * PASSES, 1 << 20, 1 << 20))])

        def middle(ap, n):
            return ap.unsqueeze(2).broadcast_to([ap.shape[0], ap.shape[1], n, ap.shape[2]])

        def last(ap, n):
            return ap.unsqueeze(len(ap.shape)).broadcast_to(list(ap.shape) + [n])

        block = ctx.enter_context(nc.Block())

        @block.sync
        def _(sp):
            def load_expert(n, v, first_pass=False):
                for i in range(PER_EXPERT):
                    if first_pass:
                        sp.wait_ge(slot_free[i], n * (S_EXP // RING) + S_EXP // RING)
                    sp.wait_ge(*once_split(before(v), i))
                    at = n * LAYER_SLOTS + (S_EXP + v.k * PER_EXPERT + i)
                    if v.pair is not None:
                        at = at + v.pair * (2 * PER_EXPERT)
                    sp.dma_start(ring[:, i, :], wring[bass.ds(at, 1)].rearrange("o p n -> (o p) n")) \
                      .then_inc(slot_full[i], 16)

            def load_others(n, w):
                with sp.Fori(0, NE // 2 - 1) as pair:
                    for k in range(1, 3):
                        load_expert(n, Visit(None, w, pair, k))
                load_expert(n, Visit(None, w, None, NE - 1))

            with sp.Fori(0, DEPTH) as n:
                sp.wait_ge(passes_counted, n + 1)
                sp.sem_inc(carried, 1)
                w = sp.value_load(tally_i[0:1, 0:1], min_val=0, max_val=DEPTH * PASSES)
                for i in range(RING):
                    sp.wait_ge(*once_split(Visit(None, w, None, -1), i))
                    sp.dma_start(ring[:, i, :], wring[bass.ds(n * LAYER_SLOTS + i, 1)].rearrange("o p n -> (o p) n")) \
                      .then_inc(slot_full[i], 16)
                with sp.Fori(1, S_EXP // RING) as m:
                    for i in range(RING):
                        sp.wait_ge(slot_free[i], n * (S_EXP // RING) + m)
                        sp.dma_start(ring[:, i, :], wring[bass.ds(n * LAYER_SLOTS + (m * RING + i), 1)]
                                     .rearrange("o p n -> (o p) n")).then_inc(slot_full[i], 16)
                load_expert(n, Visit(None, w, None, 0), first_pass=True)
                load_others(n, w)
                sp.wait_ge(passes_counted, n + 2)
                sp.sem_inc(carried, 1)
                end = sp.value_load(tally_i[0:1, 0:1], min_val=0, max_val=DEPTH * PASSES)
                with sp.If(end > w + 1):
                    with sp.Fori(w + 1, end) as more:
                        load_expert(n, Visit(None, more, None, 0))
                        load_others(n, more)

        @block.gpsimd
        def _(pool):

            pool.dma_start(x[:], x_in).then_inc(consts_loaded, 16)
            pool.dma_start(condT[:], cond).then_inc(consts_loaded, 16)
            pool.dma_start(shapes[:], shape_consts).then_inc(consts_loaded, 16)
            pool.dma_start(wr[:], w_router).then_inc(consts_loaded, 16)
            pool.dma_start(br[:], b_router.partition_broadcast(P)).then_inc(consts_loaded, 16)
            pool.dma_start(ropes[:], rope).then_inc(consts_loaded, 16)
            pool.dma_start(mask[:], na_mask).then_inc(consts_loaded, 16)
            pool.memset(conv_in[:], 0.0).then_inc(consts_made, 1)
            pool.memset(ones[:], 1.0).then_inc(consts_made, 1)
            pool.memset(half[:], -0.5).then_inc(consts_made, 1)
            for g in range(NG):
                pool.memset(tiew[:, g:g + 1], float(NG - g)).then_inc(consts_made, 1)
            pool.sem_inc(sems["x_done"], 1)

            def root(l, name, n):
                pool.wait_ge(sems["meansq_ready"], nth(l, "meansq_ready", RMS.index(name) + 1))
                pool.tensor_tensor(rstd[:, 0:n], ms[:, 0:n], half[:].broadcast_to([P, n]), ALU.pow) \
                    .then_inc(sems["rstd_ready"], 1)

            pool.wait_ge(consts_made, 3 + NG)
            with pool.Fori(0, DEPTH) as n:
                lay = bass.ds(n, 1)
                pool.wait_ge(passes_counted, n + 1)
                pool.sem_inc(carried, 1)
                l = layer_at(pool, n)
                pool.wait_ge(sems["x_done"], nth(l, "x_done", 1))
                pool.sem_inc(carried, 1)
                pool.dma_start(vecs[:], vec[lay].rearrange("o p n -> (o p) n")).then_inc(sems["small_loaded"], 16)
                pool.dma_start(rowv[:], rows[lay].rearrange("o n -> (o n)").partition_broadcast(P)) \
                    .then_inc(sems["small_loaded"], 16)
                pool.dma_start(ckvT[:, TOK:TOK + P], ckv_cache[lay].rearrange("o p n -> (o p) n")) \
                    .then_inc(sems["small_loaded"], 16)
                pool.dma_start(krc[:], kr_cache[lay].rearrange("o p n -> (o p) n")).then_inc(sems["small_loaded"], 16)
                pool.dma_start(nav[:], nav_cache[lay].rearrange("o p h n -> (o p) h n")) \
                    .then_inc(sems["small_loaded"], 16)
                for t in range(2):
                    for r in range(2):
                        first = WIN_H - 1 - (2 * t + r)
                        for h in range(NAH):
                            pool.dma_start(bias[r * GRID_W:(r + 1) * GRID_W, t, h, :].rearrange("q (j k) -> q j k", k=GRID_W), na_bias[lay, :, h, first:first + 4, :].rearrange("o q j k -> (o q) j k")) \
                                .then_inc(sems["bias_loaded"], 16)
                root(l, "norm1", TILES)
                root(l, "latent", 6)
                pool.wait_ge(sems["latents_normed"], nth(l, "latents_normed", 1))
                pool.sem_inc(carried, 1)
                pool.dma_start(new_ckv[lay].rearrange("o p n -> (o p) n"), ckvn[:, 0, :]) \
                    .then_inc(sems["latents_stored"], 16)
                root(l, "heads0", 28)
                pool.wait_ge(*once_read(l, ("proj", 6, 0)))
                pool.sem_inc(carried, 1)
                pool.dma_start(new_krope[lay].rearrange("o p n -> (o p) n"), proj[:, 0, O_KR:O_KR + ROPE]) \
                    .then_inc(sems["values_stored"], 16)
                pool.dma_start(new_nav[lay].rearrange("o p n -> (o p) n"), proj[:, 0, O_NA + 512:O_NA + 768]) \
                    .then_inc(sems["values_stored"], 16)
                pool.wait_ge(*once_read(l, ("conv", 1)))
                pool.wait_ge(sems["small_loaded"], nth(l, "small_loaded", PER_LAYER["small_loaded"]))
                for k in range(TAPS):
                    tap = vecs[:, V_TAP + 2 * k + 1:V_TAP + 2 * k + 2].broadcast_to([P, C_OUT])
                    pool.tensor_tensor(tap_product, conv_in[:, 1, k:k + C_OUT], tap, ALU.mult) \
                        .then_inc(sems["conv_steps"], 1)
                    pool.wait_ge(sems["conv_steps"], nth(l, "conv_steps", 2 * k + 1))
                    so_far = conv_acc[:, 1, :] if k else vecs[:, V_DWB + 1:V_DWB + 2].broadcast_to([P, C_OUT])
                    pool.tensor_tensor(conv_acc[:, 1, :], tap_product, so_far, ALU.add) \
                        .then_inc(sems["conv_steps"], 1)
                    pool.wait_ge(sems["conv_steps"], nth(l, "conv_steps", 2 * k + 2))
                    if k == ROOT_AT:
                        root(l, "heads1", 28)
                root(l, "heads2", 24)
                pool.wait_ge(*once_full(l, ("S", 4, 0)))
                pool.sem_inc(carried, 1)
                pool.dma_start(kT[0:NAD, 0, :, TOK:TOK + P], nak_cache[lay].rearrange("o p h n -> (o p) h n")) \
                    .then_inc(sems["na_cache_loaded"], 16)
                pool.wait_ge(sems["heads_normed"], nth(l, "heads_normed", 3))
                pool.sem_inc(carried, 1)
                pool.dma_start(new_nak[lay].rearrange("o p (h n) -> (o p) h n", h=NAH), qk[:, 3, :, 0:NAD]) \
                    .then_inc(sems["keys_stored"], 16)
                root(l, "conv", TILES)
                root(l, "norm2", TILES)
                for name in ("latents_stored", "values_stored", "keys_stored"):
                    pool.wait_ge(sems[name], nth(l, name, PER_LAYER[name]))

                def split_rest(v, i):
                    pool.wait_ge(*once_hi(v, i))
                    pool.wait_ge(*once_split_free(v, i))
                    pool.tensor_tensor(w_lo[:, split_no(v, i), :], ring[:, i, :], w_hi[:, split_no(v, i), :],
                                       ALU.subtract).then_inc(lo_made[split_no(v, i)], 1)

                pool.sem_inc(carried, 1)
                pool.memset(acc[:], 0.0).then_inc(sems["acc_cleared"], 1)

                pool.wait_ge(passes_counted, l.n + 2)
                pool.sem_inc(carried, 1)
                end = pool.value_load(tally_i[0:1, 0:1], min_val=0, max_val=DEPTH * PASSES)
                with pool.Fori(l.passes, end) as w:
                    v = Visit(l, w, None, 0)
                    split_rest(v, 1)
                    split_rest(v, 4)
                    with pool.Fori(0, NE // 2 - 1) as pair:
                        for k in range(1, 3):
                            v = Visit(l, w, pair, k)
                            split_rest(v, 1)
                            split_rest(v, 4)
                    v = Visit(l, w, None, NE - 1)
                    split_rest(v, 1)
                    split_rest(v, 4)
            pool.wait_ge(sems["x_done"], DEPTH + 1)
            pool.dma_start(y_prompt, x[:, 0, :]).then_inc(outputs_stored, 16)
            pool.dma_start(y_sample.rearrange("(t p) n -> p t n", p=P), x[:, 1:3, :]).then_inc(outputs_stored, 16)
            pool.wait_ge(outputs_stored, 32)

        @block.tensor
        def _(pe):

            def pass_over(l, n):
                pe.wait_ge(bank_read[n % BANKS], l.turns + (n // BANKS + 1))
                pe.sem_inc(bank_full[n % BANKS], 1)
                pe.sem_inc(bank_read[n % BANKS], 1)


            def turn_around(l, key, parts, d=P, frees_slot=None):
                pe.wait_ge(*once_free(l, key))
                b = bank[bank_no(l, key)]
                if d == NAD:
                    pe.sem_inc(carried, 1)
                for i, part in enumerate(parts):
                    mm = pe.transpose(b[0:d, i * P:(i + 1) * P], part, iden[:])
                    if i == 0 and frees_slot is not None:
                        mm.then_inc(slot_free[frees_slot % RING], 1)
                mm.then_inc(bank_full[bank_no(l, key)], 1)

            def project(l, j, frees_slot=None):
                n = 256 if j < IN_SLOTS - 1 else LAST_W
                pe.wait_ge(*once_loaded(l, S_IN + j))
                w = ring[:, (S_IN + j) % RING, :][:, 0:KC * n].rearrange("p (k n) -> p k n", k=KC)
                for t in range(TILES):
                    pe.wait_ge(*once_free(l, ("proj", j, t)))
                    b = bank[bank_no(l, ("proj", j, t))]
                    for c in range(KC):
                        mm = pe.matmul(b[:, 0:n], hT[:, c, t * P:(t + 1) * P], w[:, c, :],
                                       start=(c == 0), stop=(c == KC - 1))
                        if c == 0 and t == 0 and frees_slot is not None:
                            mm.then_inc(slot_free[frees_slot % RING], 1)
                    mm.then_inc(bank_full[bank_no(l, ("proj", j, t))], 1)

            def queries(l, p):
                pe.wait_ge(*once_loaded(l, S_UP))
                w = ring[:, S_UP % RING, :][:, 0:2 * 768].rearrange("p (k n) -> p k n", k=2)
                for t in range(TILES):
                    pe.wait_ge(*once_free(l, ("q", p, t)))
                    b = bank[bank_no(l, ("q", p, t))]
                    for c in range(2):
                        mm = pe.matmul(b[:, 0:384], qlatT[:, c, t * P:(t + 1) * P], w[:, c, p * 384:(p + 1) * 384],
                                       start=(c == 0), stop=(c == 1))
                    mm.then_inc(bank_full[bank_no(l, ("q", p, t))], 1)

            def keys_values(l, p):
                if p == 0:
                    pe.wait_ge(*once_loaded(l, S_UP))
                    w = ring[:, S_UP % RING, :][:, 1536:2048]
                else:
                    pe.wait_ge(*once_loaded(l, S_UP - 1))
                    w = ring[:, (S_UP - 1) % RING, :][:, KC * LAST_W:KC * LAST_W + 512]
                for t in range(4):
                    pe.wait_ge(*once_free(l, ("kv", p, t)))
                    b = bank[bank_no(l, ("kv", p, t))]
                    mm = pe.matmul(b[:, :], ckvT[:, t * P:(t + 1) * P], w, start=True, stop=True)
                    mm.then_inc(bank_full[bank_no(l, ("kv", p, t))], 1)

            def turn_heads(l, p):
                d = QKD if p < 2 else NAD
                pe.wait_ge(sems["heads_normed"], nth(l, "heads_normed", p + 1))
                for h in range(4):
                    turn_around(l, ("qT", p, h), [qk[:, t, h, 0:d] for t in range(3)], d)
                    turn_around(l, ("kT", p, h), [qk[:, 3 + t, h, 0:d] for t in range(4 if p < 2 else 3)], d)

            def scores(l, g):
                p, h = GROUPS[g]
                d, s = (QKD if p < 2 else NAD), p % 2
                pe.wait_ge(*once_read(l, ("qT", p, h)))
                pe.wait_ge(*once_read(l, ("kT", p, h)))
                if g == 8:
                    pe.wait_ge(sems["na_cache_loaded"], nth(l, "na_cache_loaded", 16))
                pe.sem_inc(carried, 1)
                for t in range(TILES):
                    pe.wait_ge(*once_free(l, ("S", g, t)))
                    b = bank[bank_no(l, ("S", g, t))]
                    lo, hi = (0, P) if t == 0 else (P, 4 * P)
                    mm = pe.matmul(b[:, 0:hi - lo], qT[0:d, s, h, t * P:(t + 1) * P], kT[0:d, s, h, lo:hi],
                                   start=True, stop=True)
                    mm.then_inc(bank_full[bank_no(l, ("S", g, t))], 1)

            def turn_probs(l, g):
                if GROUPS[g][0] < 2:
                    pe.wait_ge(*once_read(l, ("S", g, 2)))
                else:
                    pe.wait_ge(sems["na_exp_done"], nth(l, "na_exp_done", 2 * GROUPS[g][1] + 2))
                part = [probs[:, g % 2, k * P:(k + 1) * P] for k in range(7)]
                pe.wait_ge(*once_free(l, ("PT", g, 0)))
                b = bank[bank_no(l, ("PT", g, 0))]
                for k in range(4):
                    mm = pe.transpose(b[:, k * P:(k + 1) * P], part[k], iden[:])
                    if g == 0 and k < 2:
                        mm.then_inc(slot_free[(S_UP - 1 + k) % RING], 1)
                mm.then_inc(bank_full[bank_no(l, ("PT", g, 0))], 1)
                turn_around(l, ("PT", g, 1), part[4:])

            def values(l, g):
                p, h = GROUPS[g]
                pe.wait_ge(*once_read(l, ("PT", g, 0)))
                pe.wait_ge(*once_read(l, ("PT", g, 1)))
                pe.wait_ge(*once_free(l, ("O", g)))
                b = bank[bank_no(l, ("O", g))]
                for t in range(TILES):
                    keys = [0] if t == 0 else [1, 2, 3]
                    for i, k in enumerate(keys):
                        col = 0 if t == 0 else 1 + 3 * (t - 1) + i
                        if p < 2:
                            v = v_mla[:, k, 4 * p + h, :]
                        elif k == 3:
                            v = nav[:, h, :]
                        else:
                            v = proj[:, k, O_NA + 512 + h * NAD:O_NA + 512 + (h + 1) * NAD]
                        mm = pe.matmul(b[:, t * VD:(t + 1) * VD], probsT[:, g % 2, col * P:(col + 1) * P], v,
                                       start=(i == 0), stop=(i == len(keys) - 1))
                mm.then_inc(bank_full[bank_no(l, ("O", g))], 1)

            def gate_rows(l, what, m):
                for c in range(2):
                    for n in range(2):
                        pe.wait_ge(*once_free(l, (what, c, n)))
                        b = bank[bank_no(l, (what, c, n))]
                        for i in range(4):
                            mm = pe.matmul(b[:, i * P:(i + 1) * P],
                                           modT[:, m, 4 * n + i, c:c + 1].broadcast_to([P, P]),
                                           iden[:], start=True, stop=True)
                        mm.then_inc(bank_full[bank_no(l, (what, c, n))], 1)

            def turn_mod(l, m):
                pe.wait_ge(*once_read(l, ("ada", 4 * m + 3)))
                pe.wait_ge(*once_free(l, ("mod", m)))
                b = bank[bank_no(l, ("mod", m))]
                pe.sem_inc(carried, 1)
                for c in range(KC):
                    mm = pe.transpose(b[:, 2 * c:2 * c + 2], modrow[:, m % 2, c * P:(c + 1) * P], iden[0:2, 0:2])
                mm.then_inc(bank_full[bank_no(l, ("mod", m))], 1)

            for i in range(BANKS):
                pe.sem_inc(bank_read[i], 1)
            pe.wait_ge(consts_loaded, N_CONST)
            pe.wait_ge(cond_ready, 1)
            with pe.Fori(0, DEPTH) as n:
                pe.wait_ge(passes_counted, n + 1)
                pe.sem_inc(carried, 1)
                l = layer_at(pe, n)
                for s in range(ADA_SLOTS):
                    pe.wait_ge(*once_loaded(l, s))
                    w = ring[:, s % RING, :].rearrange("p (k n) -> p k n", k=KC)
                    pe.wait_ge(*once_free(l, ("ada", s)))
                    b = bank[bank_no(l, ("ada", s))]
                    for c in range(KC):
                        mm = pe.matmul(b[0:2, 0:256], condT[:, c, :], w[:, c, :], start=(c == 0), stop=(c == KC - 1))
                        if c == 0 and s:
                            mm.then_inc(slot_free[(s - 1) % RING], 1)
                    mm.then_inc(bank_full[bank_no(l, ("ada", s))], 1)
                    if s % 4 == 0 and s:
                        turn_mod(l, s // 4 - 1)
                turn_mod(l, 5)
                pe.wait_ge(sems["normed_tile"], nth(l, "normed_tile", TILES))
                for c in range(KC):
                    turn_around(l, ("n1", c), [xn[:, t, c * P:(c + 1) * P] for t in range(TILES)],
                                frees_slot=ADA_SLOTS - 1 if c == 0 else None)
                pe.wait_ge(*once_read(l, ("n1", 6)))
                pe.wait_ge(*once_read(l, ("n1", 7)))
                for j in range(4):
                    project(l, j, S_IN + j - 1 if j else None)
                pe.wait_ge(sems["latents_normed"], nth(l, "latents_normed", 1))
                for c in range(2):
                    turn_around(l, ("ql", c), [q_lat_n[:, t, c * P:(c + 1) * P] for t in range(TILES)],
                                frees_slot=S_IN + 3 if c == 0 else None)
                turn_around(l, ("ckv",), [ckvn[:, t, :] for t in range(TILES)])
                project(l, 4)
                pe.wait_ge(sems["glu_ready"], nth(l, "glu_ready", 1))
                for c in range(2):
                    turn_around(l, ("conv", c), [glu[:, t, c * P:(c + 1) * P] for t in range(TILES)],
                                frees_slot=S_IN + 4 if c == 0 else None)
                pe.wait_ge(*once_read(l, ("ql", 1)))
                pe.wait_ge(*once_read(l, ("ckv",)))
                pe.wait_ge(sems["small_loaded"], nth(l, "small_loaded", PER_LAYER["small_loaded"]))
                queries(l, 0)
                keys_values(l, 0)
                project(l, 5)
                project(l, 6, S_IN + 5)
                turn_heads(l, 0)
                queries(l, 1)
                keys_values(l, 1)
                for i in range(len(GROUPS) + 2):
                    if i < len(GROUPS):
                        scores(l, i)
                    if 1 <= i <= len(GROUPS):
                        turn_probs(l, i - 1)
                    if i >= 2:
                        values(l, i - 2)
                    if i == 3:
                        turn_heads(l, 1)
                    if i == 7:
                        turn_heads(l, 2)
                    if i == 9:
                        pe.wait_ge(sems["conv_lower"], nth(l, "conv_lower", 1))
                        pe.wait_ge(sems["conv_steps"], nth(l, "conv_steps", 2 * TAPS))
                        for t in range(TILES):
                            at = 0 if t == 0 else C_LAT - PAD + (t - 1) * P
                            turn_around(l, ("cb", t), [conv_acc[:, c, at:at + P] for c in range(2)])
                    if i == 10:
                        pe.wait_ge(*once_read(l, ("cb", 2)))
                        for c in range(2):
                            turn_around(l, ("ln", c), [ln_tm[:, t, c * P:(c + 1) * P] for t in range(TILES)])
                gate_rows(l, "g1", 2)
                pe.wait_ge(*once_read(l, ("O", len(GROUPS) - 1)))
                for c in range(6):
                    turn_around(l, ("mix", c), [xn[:, t, c * P:(c + 1) * P] for t in range(TILES)])
                pe.wait_ge(*once_read(l, ("mix", 5)))
                pe.wait_ge(sems["conv_mixed"], nth(l, "conv_mixed", 1))
                for j in range(OUT_SLOTS):
                    pe.wait_ge(*once_loaded(l, S_OUT + j))
                    w = ring[:, (S_OUT + j) % RING, :].rearrange("p (k n) -> p k n", k=KC)
                    for t in range(TILES):
                        pe.wait_ge(*once_free(l, ("out", j, t)))
                        b = bank[bank_no(l, ("out", j, t))]
                        for c in range(KC):
                            mm = pe.matmul(b[:, 0:256], hT[:, c, t * P:(t + 1) * P], w[:, c, :],
                                           start=(c == 0), stop=(c == KC - 1))
                            if j and t == 0 and c == 0:
                                mm.then_inc(slot_free[(S_OUT + j - 1) % RING], 1)
                        mm.then_inc(bank_full[bank_no(l, ("out", j, t))], 1)
                pe.wait_ge(sems["normed_tile"], nth(l, "normed_tile", 2 * TILES))
                for c in range(KC):
                    turn_around(l, ("n2", c), [xn[:, t, c * P:(c + 1) * P] for t in range(TILES)],
                                frees_slot=S_EXP - 1 if c == 0 else None)
                pe.wait_ge(*once_read(l, ("n2", 6)))
                pe.wait_ge(*once_read(l, ("n2", 7)))
                pe.wait_ge(*once_free(l, ("router",)))
                b = bank[bank_no(l, ("router",))]
                for t in range(TILES):
                    for c in range(KC):
                        mm = pe.matmul(b[:, t * NE:(t + 1) * NE], hT[:, c, t * P:(t + 1) * P], wr[:, c, :],
                                       start=(c == 0), stop=(c == KC - 1))
                mm.then_inc(bank_full[bank_no(l, ("router",))], 1)
                for t in range(TILES):
                    for q in range(2):
                        turn_around(l, ("h", t, q), [hT[:, 4 * q + i, t * P:(t + 1) * P] for i in range(4)])
                pe.wait_ge(sems["chosen"], nth(l, "chosen", 1))
                pe.wait_ge(*once_free(l, ("place",)))
                b = bank[bank_no(l, ("place",))]
                for t in range(TILES + 1):
                    for k in range(min(t + 1, TILES)):
                        mm = pe.matmul(b[:, t * NE:(t + 1) * NE], shapes[:, 2, :] if k == t else ones[:].broadcast_to([P, P]),
                                       chosen[:, k * NE:(k + 1) * NE], start=(k == 0), stop=(k == min(t, TILES - 1)))
                mm.then_inc(bank_full[bank_no(l, ("place",))], 1)
                gate_rows(l, "g2", 5)
                for n in range(SPARE):
                    pass_over(l, len(PLAN) + n)

                def products(b, hi, lo, v, i, at, start, stop, key, frees_before=None, frees_here=False):
                    q = split_no(v, i)
                    w = (w_hi[:, q, at:at + 512], w_lo[:, q, at:at + 512])
                    for k, (a, m) in enumerate(((hi, 0), (lo, 0), (hi, 1))):
                        mm = pe.matmul(b[:, :], a, w[m], start=(start and k == 0), stop=(stop and k == 2))
                        if k == 0 and frees_before is not None:
                            mm.then_inc(split_used[split_no(v, frees_before)], 1)
                    if stop:
                        mm.then_inc(bank_full[bank_no(v, key)], 1)
                    elif frees_here:
                        mm.then_inc(split_used[q], 1)

                def gather(v, first=False):
                    pe.wait_ge(pick_made, visits(v, 1, 1))
                    for k in range(4):
                        pe.wait_ge(*once_free(v, ("gather", k)))
                        b = bank[bank_no(v, ("gather", k))]
                        h = (h_hi, h_lo)[k % 2]
                        for i in range(4):
                            c = 4 * (k // 2) + i
                            for t in range(TILES):
                                mm = pe.matmul(b[:, i * P:(i + 1) * P], h[:, t, c * P:(c + 1) * P], pick[:, t, :],
                                               start=(t == 0), stop=(t == TILES - 1))
                                if not first and (k, i, t) == (0, 0, 0):
                                    mm.then_inc(split_used[split_no(before(v), 5)], 1)
                        mm.then_inc(bank_full[bank_no(v, ("gather", k))], 1)
                    pe.wait_ge(*once_free(v, ("ST",)))
                    b = bank[bank_no(v, ("ST",))]
                    for t in range(TILES):
                        mm = pe.matmul(b[:, t * P:(t + 1) * P], pick[:, t, :], iden_r[:], start=True, stop=True)
                    mm.then_inc(bank_full[bank_no(v, ("ST",))], 1)

                def gate_up(v):
                    for what, s in (("G", 0), ("U", 2)):
                        pe.wait_ge(*once_free(v, (what,)))
                        b = bank[bank_no(v, (what,))]
                        for i in range(2):
                            pe.wait_ge(*once_split(v, s + i))
                            if s == 0:
                                pe.wait_ge(*once_read(v, ("gather", 2 * i)))
                                pe.wait_ge(*once_read(v, ("gather", 2 * i + 1)))
                            for c in range(4):
                                products(b, hg_hi[:, 4 * i + c, :], hg_lo[:, 4 * i + c, :], v, s + i, c * 512,
                                         (i, c) == (0, 0), (i, c) == (1, 3), (what,),
                                         frees_before=1 if (s, i, c) == (2, 0, 0) else None,
                                         frees_here=(i, c) == (0, 3))

                def turn_hidden(v, frees=None):
                    pe.wait_ge(*once_read(v, ("U",)))
                    pe.wait_ge(*once_free(v, ("T",)))
                    b = bank[bank_no(v, ("T",))]
                    for c in range(FC):
                        mm = pe.transpose(b[:, c * P:(c + 1) * P], sg[:, c * P:(c + 1) * P], iden[:])
                        if frees is not None and c == 0:
                            mm.then_inc(split_used[frees], 1)
                    mm.then_inc(bank_full[bank_no(v, ("T",))], 1)

                def scatter(v, turns, frees=None):
                    if turns[0] == 0:
                        pe.wait_ge(*once_read(v, ("ST",)))
                        pe.wait_ge(*once_read(v, ("Y", 0)))
                        pe.wait_ge(*once_read(v, ("Y", 1)))
                    for k in turns:
                        t, n = k // 2, k % 2
                        pe.wait_ge(*once_free(v, ("scatter", k)))
                        b = bank[bank_no(v, ("scatter", k))]
                        pt = pickT[:, v.k % 2, t * P:(t + 1) * P]
                        mm = pe.matmul(b[:, :], pt, y_hi[:, n * 512:(n + 1) * 512], start=True, stop=False)
                        if frees is not None and k == 0:
                            mm.then_inc(split_used[frees], 1)
                        mm = pe.matmul(b[:, :], pt, y_lo[:, n * 512:(n + 1) * 512], start=False, stop=True)
                        mm.then_inc(bank_full[bank_no(v, ("scatter", k))], 1)

                def down(v):
                    pe.wait_ge(*once_read(v, ("T",)))
                    y = []
                    for n in range(2):
                        pe.wait_ge(*once_free(v, ("Y", n)))
                        y.append(bank[bank_no(v, ("Y", n))])
                    for i in range(2):
                        pe.wait_ge(*once_split(v, 4 + i))
                        for c in range(2):
                            for n in range(2):
                                products(y[n], hidT_hi[:, 2 * i + c, :], hidT_lo[:, 2 * i + c, :], v, 4 + i,
                                         c * D_MODEL + n * 512, (i, c) == (0, 0), (i, c) == (1, 1), ("Y", n),
                                         frees_here=(i, c, n) == (0, 1, 1))

                def step_expert(v):
                    if v.pair is not None:
                        scatter(before(v), range(SCAT // 2), frees=split_no(v, 3))
                        turn_hidden(v)
                        scatter(before(v), range(SCAT // 2, SCAT))
                    else:
                        turn_hidden(v, frees=split_no(v, 3))
                    down(v)
                    gather(after(v))
                    gate_up(after(v))

                pe.wait_ge(passes_counted, l.n + 2)
                pe.sem_inc(carried, 1)
                end = pe.value_load(tally_i[0:1, 0:1], min_val=0, max_val=DEPTH * PASSES)
                for t in range(TILES):
                    pe.wait_ge(*once_read(l, ("h", t, 1)))
                pe.sem_inc(carried, 1)
                with pe.Fori(l.passes, end) as w:
                    gather(Visit(l, w, None, 0), first=True)
                    gate_up(Visit(l, w, None, 0))
                    step_expert(Visit(l, w, None, 0))
                    with pe.Fori(0, NE // 2 - 1) as pair:
                        for k in range(1, 3):
                            step_expert(Visit(l, w, pair, k))
                    last_one = Visit(l, w, None, NE - 1)
                    scatter(before(last_one), range(SCAT // 2), frees=split_no(last_one, 3))
                    turn_hidden(last_one)
                    scatter(before(last_one), range(SCAT // 2, SCAT))
                    down(last_one)
                    scatter(last_one, range(SCAT), frees=split_no(last_one, 5))

        @block.scalar
        def _(act):
            def square_sums(l, k):
                for t in range(TILES):
                    if k == 2:
                        act.wait_ge(sems["x_mid"], nth(l, "x_mid", t + 1))
                    ins = act.activation(xn[:, t, :], x[:, t, :], ACT.Square, accum_out=ssum[:, t:t + 1])
                ins.then_inc(sems["squares_ready"], 1)

            def modulate(l, what, a, m):
                for c in range(1, KC, 2):
                    act.wait_ge(*once_full(l, (what, c)))
                    b = bank[bank_no(l, (what, c))]
                    for q, (lo, hi) in enumerate(((0, P), (P, TOK))):
                        ins = act.activation(hT[:, c, lo:hi], b[:, lo:hi], ACT.Identity,
                                             bias=modT[:, m, c, q:q + 1], scale=a[:, c, q:q + 1])
                    ins.then_inc(bank_read[bank_no(l, (what, c))], 1)

            def evac_proj(l, j):
                n = 256 if j < IN_SLOTS - 1 else LAST_W
                for t in range(TILES):
                    act.wait_ge(*once_full(l, ("proj", j, t)))
                    b = bank[bank_no(l, ("proj", j, t))]
                    act.copy(proj[:, t, j * 256:j * 256 + n], b[:, 0:n]) \
                        .then_inc(bank_read[bank_no(l, ("proj", j, t))], 1)

            def evac_heads(l, p):
                for t in range(TILES):
                    act.wait_ge(*once_full(l, ("q", p, t)))
                    b = bank[bank_no(l, ("q", p, t))]
                    act.copy(qk[:, t, :, :].rearrange("p h n -> p (h n)"), b[:, 0:384]) \
                        .then_inc(bank_read[bank_no(l, ("q", p, t))], 1)
                for t in range(4):
                    act.wait_ge(*once_full(l, ("kv", p, t)))
                    b = bank[bank_no(l, ("kv", p, t))][:, :].rearrange("p (h n) -> p h n", h=4)
                    act.copy(v_mla[:, t, 4 * p:4 * p + 4, :], b[:, :, NOPE:])
                    act.copy(qk[:, 3 + t, :, 0:NOPE], b[:, :, 0:NOPE]) \
                        .then_inc(bank_read[bank_no(l, ("kv", p, t))], 1)

            def evac_turned(l, p):
                d, s = (QKD if p < 2 else NAD), p % 2
                for h in range(4):
                    act.wait_ge(*once_full(l, ("qT", p, h)))
                    b = bank[bank_no(l, ("qT", p, h))]
                    act.copy(qT[0:d, s, h, :], b[0:d, 0:TOK]).then_inc(bank_read[bank_no(l, ("qT", p, h))], 1)
                    n = 4 * P if p < 2 else TOK
                    act.wait_ge(*once_full(l, ("kT", p, h)))
                    b = bank[bank_no(l, ("kT", p, h))]
                    act.copy(kT[0:d, s, h, 0:n], b[0:d, 0:n]).then_inc(bank_read[bank_no(l, ("kT", p, h))], 1)

            def exponentials(l, g):
                p, h = GROUPS[g]
                act.wait_ge(sems["negmax_ready"], nth(l, "negmax_ready", g + 1))
                for t in range(TILES):
                    lo, hi = (0, P) if t == 0 else (P + (t - 1) * TOK, P + t * TOK)
                    out = probs[:, g % 2, lo:hi]
                    if p == 2 and t:
                        act.activation(out, biased[:, g % 2, t - 1, :], ACT.Exp, bias=negmax[:, g, t:t + 1],
                                       accum_out=rowsum[:, g, t:t + 1]).then_inc(sems["na_exp_done"], 1)
                    else:
                        act.wait_ge(*once_full(l, ("S", g, t)))
                        b = bank[bank_no(l, ("S", g, t))]
                        act.activation(out, b[:, 0:hi - lo], ACT.Exp, bias=negmax[:, g, t:t + 1],
                                             scale=MLA_SCALE if p < 2 else 1.0,
                                             accum_out=rowsum[:, g, t:t + 1]) \
                                                 .then_inc(bank_read[bank_no(l, ("S", g, t))], 1)

            def evac_probs(l, g):
                act.wait_ge(*once_full(l, ("PT", g, 1)))
                b = bank[bank_no(l, ("PT", g, 1))]
                act.copy(probsT[:, g % 2, 4 * P:7 * P], b[:, 0:TOK]).then_inc(bank_read[bank_no(l, ("PT", g, 1))], 1)

            def evac_gates(l, what):
                for c in range(2):
                    for n in range(2):
                        act.wait_ge(*once_full(l, (what, c, n)))
                        b = bank[bank_no(l, (what, c, n))]
                        act.copy(G[:, c, n * 512:(n + 1) * 512], b[:, :]) \
                            .then_inc(bank_read[bank_no(l, (what, c, n))], 1)

            act.wait_ge(consts_loaded, N_CONST)
            act.activation(cond_e[:], condT[:], ACT.Exp, scale=-1.0).then_inc(cond_exp, 1)
            with act.Fori(0, DEPTH) as n:
                act.wait_ge(passes_counted, n + 1)
                act.sem_inc(carried, 1)
                l = layer_at(act, n)
                act.wait_ge(sems["x_done"], nth(l, "x_done", 1))
                square_sums(l, 1)
                for s in range(ADA_SLOTS):
                    if s % 4 == 0 and s >= 8:
                        act.wait_ge(*once_full(l, ("mod", s // 4 - 2)))
                    act.wait_ge(*once_full(l, ("ada", s)))
                    b = bank[bank_no(l, ("ada", s))]
                    act.copy(modrow[:, (s // 4) % 2, (s % 4) * 256:(s % 4 + 1) * 256], b[0:2, 0:256]) \
                        .then_inc(bank_read[bank_no(l, ("ada", s))], 1)
                act.wait_ge(sems["mod_ready"], nth(l, "mod_ready", 2))
                modulate(l, "n1", a1, 0)
                for j in range(2):
                    evac_proj(l, j)
                for j in range(2, 4):
                    evac_proj(l, j)
                act.wait_ge(*once_read(l, ("proj", 3, 2)))
                act.activation(proj[:, :, O_G:O_G + CONV_CH], proj[:, :, O_G:O_G + CONV_CH], ACT.Sigmoid) \
                    .then_inc(sems["gate_sigmoid"], 1)
                evac_proj(l, 4)
                evac_heads(l, 0)
                evac_proj(l, 5)
                evac_proj(l, 6)
                evac_turned(l, 0)
                evac_heads(l, 1)
                for i in range(len(GROUPS) + 2):
                    if i < len(GROUPS):
                        exponentials(l, i)
                    if 1 <= i <= len(GROUPS):
                        evac_probs(l, i - 1)
                    if i == 3:
                        evac_turned(l, 1)
                    if i == 7:
                        evac_turned(l, 2)
                evac_gates(l, "g1")
                for c in range(6):
                    act.wait_ge(*once_full(l, ("mix", c)))
                    b = bank[bank_no(l, ("mix", c))]
                    act.copy(hT[:, c if c < 4 else c + 2, :], b[:, 0:TOK]) \
                        .then_inc(bank_read[bank_no(l, ("mix", c))], 1)
                act.wait_ge(*once_read(l, ("ln", 1)))
                act.activation(hT[:, 4:6, :], z_conv, ACT.Silu).then_inc(sems["conv_mixed"], 1)
                square_sums(l, 2)
                modulate(l, "n2", a2, 3)
                act.wait_ge(*once_full(l, ("router",)))
                b = bank[bank_no(l, ("router",))]
                act.activation(aff[:], b[:, 0:TILES * NE], ACT.Sigmoid) \
                    .then_inc(bank_read[bank_no(l, ("router",))], 1)
                for name in ("latents_stored", "values_stored", "keys_stored"):
                    act.wait_ge(sems[name], nth(l, name, PER_LAYER[name]))
                act.copy(iden_r[:], iden)
                for t in range(TILES):
                    for q in range(2):
                        act.wait_ge(*once_full(l, ("h", t, q)))
                        b = bank[bank_no(l, ("h", t, q))]
                        act.copy(h_hi[:, t, q * 512:(q + 1) * 512], b[:, :]).then_inc(sems["h_hi_made"], 1)
                evac_gates(l, "g2")

                def split_high(v, i):
                    act.wait_ge(*expert_loaded(v, i))
                    act.wait_ge(*once_split_free(v, i))
                    act.copy(w_hi[:, split_no(v, i), :], ring[:, i, :]).then_inc(hi_made[split_no(v, i)], 1)

                def gathered_high(v):
                    for k in (0, 2):
                        act.wait_ge(*once_full(v, ("gather", k)))
                        b = bank[bank_no(v, ("gather", k))]
                        act.copy(hg_hi[:, 2 * k:2 * k + 4, :].rearrange("p c n -> p (c n)"), b[:, :]) \
                            .then_inc(bank_read[bank_no(v, ("gather", k))], 1)
                    act.wait_ge(*once_full(v, ("ST",)))
                    b = bank[bank_no(v, ("ST",))]
                    act.copy(pickT[:, v.k % 2, :], b[:, 0:TOK]).then_inc(bank_read[bank_no(v, ("ST",))], 1)

                def silu_gate(v):
                    act.wait_ge(*once_full(v, ("G",)))
                    b = bank[bank_no(v, ("G",))]
                    act.activation(sg[:], b[:, :], ACT.Silu).then_inc(bank_read[bank_no(v, ("G",))], 1)

                def finish_expert(v, follows=True):
                    if follows:
                        split_high(after(v), 0)
                    act.wait_ge(*once_full(v, ("T",)))
                    b = bank[bank_no(v, ("T",))]
                    act.copy(hidT_hi[:, :, :].rearrange("p c n -> p (c n)"), b[:, :]).then_inc(hidT_hi_made, 1)
                    if follows:
                        split_high(after(v), 1)
                        split_high(after(v), 2)
                    for n in range(2):
                        act.wait_ge(*once_full(v, ("Y", n)))
                        b = bank[bank_no(v, ("Y", n))]
                        act.copy(y_hi[:, n * 512:(n + 1) * 512], b[:, :]).then_inc(y_hi_made, 1)
                    if follows:
                        gathered_high(after(v))
                        split_high(after(v), 3)
                        split_high(after(v), 4)
                        silu_gate(after(v))
                        split_high(after(v), 5)

                act.wait_ge(passes_counted, l.n + 2)
                act.sem_inc(carried, 1)
                end = act.value_load(tally_i[0:1, 0:1], min_val=0, max_val=DEPTH * PASSES)
                with act.Fori(l.passes, end) as w:
                    v = Visit(l, w, None, 0)
                    split_high(v, 0)
                    split_high(v, 1)
                    gathered_high(v)
                    for i in range(2, 5):
                        split_high(v, i)
                    silu_gate(v)
                    split_high(v, 5)
                    finish_expert(v)
                    with act.Fori(0, NE // 2 - 1) as pair:
                        for k in range(1, 3):
                            finish_expert(Visit(l, w, pair, k))
                    finish_expert(Visit(l, w, None, NE - 1), follows=False)

        @block.vector
        def _(dve):
            count = [0]

            def step(l):
                count[0] += 1
                return nth(l, "dve_step", count[0])

            def mean_squares(l, name, n, width):
                k = RMS.index(name) + 1
                dve.tensor_scalar(ms[:, 0:n], ssum[:, 0:n], 1.0 / width, EPS, ALU.mult, ALU.add) \
                    .then_inc(sems["meansq_ready"], 1)
                dve.wait_ge(sems["meansq_ready"], nth(l, "meansq_ready", k))

            def normalise(l, name, k):
                dve.wait_ge(sems["squares_ready"], nth(l, "squares_ready", k))
                mean_squares(l, name, TILES, D_MODEL)
                dve.wait_ge(sems["rstd_ready"], nth(l, "rstd_ready", RMS.index(name) + 1))
                for t in range(TILES):
                    dve.tensor_scalar(xn[:, t, :], x[:, t, :], rstd[:, t:t + 1], None, ALU.mult) \
                        .then_inc(sems["normed_tile"], 1)
                    dve.wait_ge(sems["normed_tile"], nth(l, "normed_tile", TILES * (k - 1) + t + 1))

            def modulate(l, what, a, m):
                for c in range(0, KC, 2):
                    dve.wait_ge(*once_full(l, (what, c)))
                    b = bank[bank_no(l, (what, c))]
                    for q, (lo, hi) in enumerate(((0, P), (P, TOK))):
                        ins = dve.tensor_scalar(hT[:, c, lo:hi], b[:, lo:hi], a[:, c, q:q + 1],
                                                modT[:, m, c, q:q + 1], ALU.mult, ALU.add)
                    ins.then_inc(bank_read[bank_no(l, (what, c))], 1)

            def head_sums(l, p):
                if p < 2:
                    if p == 1:
                        dve.wait_ge(*once_full(l, ("kT", 0, 3)))
                    for t in range(4):
                        src = proj[:, t, O_KR:O_KR + ROPE] if t < 3 else krc[:]
                        dve.tensor_copy(qk[:, 3 + t, :, NOPE:], src.unsqueeze(1).broadcast_to([P, 4, ROPE])) \
                            .then_inc(sems["dve_step"], 1)
                        dve.wait_ge(sems["dve_step"], step(l))
                    dve.wait_ge(*once_read(l, ("q", p, 2)))
                    for lo, hi in ((0, 3), (3, 7)):
                        if lo:
                            dve.wait_ge(*once_read(l, ("kv", p, 3)))
                        m = (hi - lo) * 4
                        dve.tensor_tensor(squares[:, 0:m * QKD], flat(qk[:, lo:hi, :, :]),
                                                 flat(qk[:, lo:hi, :, :]), ALU.mult).then_inc(sems["dve_step"], 1)
                        dve.wait_ge(sems["dve_step"], step(l))
                        dve.tensor_reduce(ssum[:, lo * 4:hi * 4],
                                                 squares[:, 0:m * QKD].rearrange("p (a n) -> p a n", n=QKD), AX, ALU.add) \
                                                     .then_inc(sems["dve_step"], 1)
                        dve.wait_ge(sems["dve_step"], step(l))
                    mean_squares(l, f"heads{p}", 28, QKD)
                else:
                    dve.wait_ge(*once_read(l, ("proj", 5, 2)))
                    src = proj[:, :, O_NA:O_NA + 512]
                    dve.tensor_tensor(squares[:, :].rearrange("p (t n) -> p t n", t=3), src, src, ALU.mult) \
                        .then_inc(sems["dve_step"], 1)
                    dve.wait_ge(sems["dve_step"], step(l))
                    dve.tensor_reduce(ssum[:, 0:24], squares[:, :].rearrange("p (a n) -> p a n", n=NAD), AX, ALU.add) \
                        .then_inc(sems["dve_step"], 1)
                    dve.wait_ge(sems["dve_step"], step(l))
                    mean_squares(l, "heads2", 24, NAD)

            def head_gains(l, p):
                if p < 2:
                    for lo, hi, at in ((0, 3, R_Q), (3, 7, R_K)):
                        v = qk[:, lo:hi, :, :].rearrange("p t h n -> p (t h) n")
                        g = rowv[:, at:at + QKD].unsqueeze(1).broadcast_to([P, (hi - lo) * 4, QKD])
                        dve.tensor_tensor(v, v, g, ALU.mult).then_inc(sems["dve_step"], 1)
                        dve.wait_ge(sems["dve_step"], step(l))
                    cos, sin = ropes[:, :, 0, :], ropes[:, :, 1, :]
                    m1 = turned[:, 0, :].rearrange("p (t h n) -> p t h n", t=2, h=4)
                    m2 = turned[:, 1, :].rearrange("p (t h n) -> p t h n", t=2, h=4)
                    for lo in (1, 4):
                        v = qk[:, lo:lo + 2, :, NOPE:]
                        dve.tensor_tensor(m1, v, middle(cos, 4), ALU.mult)
                        dve.tensor_tensor(m2[:, :, :, 0::2], v[:, :, :, 1::2], middle(sin[:, :, 0::2], 4), ALU.mult)
                        dve.tensor_tensor(m2[:, :, :, 1::2], v[:, :, :, 0::2], middle(sin[:, :, 1::2], 4),
                                                 ALU.mult).then_inc(sems["dve_step"], 1)
                        dve.wait_ge(sems["dve_step"], step(l))
                        dve.tensor_tensor(v, m1, m2, ALU.add).then_inc(sems["dve_step"], 1)
                        dve.wait_ge(sems["dve_step"], step(l))
                else:
                    dve.wait_ge(*once_full(l, ("kT", 1, 3)))
                    for q, at in enumerate((R_NQ, R_NK)):
                        dve.tensor_tensor(
                            qk[:, 3 * q:3 * q + 3, :, 0:NAD],
                            proj[:, :, O_NA + 256 * q:O_NA + 256 * (q + 1)].rearrange("p t (h n) -> p t h n", h=4),
                            rowv[:, at:at + NAD].unsqueeze(1).unsqueeze(1).broadcast_to([P, TILES, 4, NAD]), ALU.mult) \
                                .then_inc(sems["dve_step"], 1)
                        dve.wait_ge(sems["dve_step"], step(l))

            def head_scales(l, p):
                dve.wait_ge(sems["rstd_ready"], nth(l, "rstd_ready", RMS.index(f"heads{p}") + 1))
                if p < 2:
                    rows_ = qk[:, :, :, :].rearrange("p t h n -> p (t h) n")
                    ins = dve.tensor_tensor(rows_, rows_, last(rstd[:, 0:28], QKD), ALU.mult)
                else:
                    r = rstd[:, 0:24].rearrange("p (t a) -> p t a", t=3)
                    dve.tensor_scalar(r[:, :, 0:4], r[:, :, 0:4], NA_SCALE, None, ALU.mult) \
                        .then_inc(sems["dve_step"], 1)
                    dve.wait_ge(sems["dve_step"], step(l))
                    for q in range(2):
                        v = qk[:, 3 * q:3 * q + 3, :, 0:NAD]
                        ins = dve.tensor_tensor(v, v, last(r[:, :, 4 * q:4 * q + 4], NAD), ALU.mult)
                ins.then_inc(sems["heads_normed"], 1)
                dve.wait_ge(sems["heads_normed"], nth(l, "heads_normed", p + 1))

            def flat(ap):
                return ap.rearrange("p t h n -> p (t h n)")

            def maxima(l, g):
                p, h = GROUPS[g]
                for t in range(TILES):
                    dve.wait_ge(*once_full(l, ("S", g, t)))
                    b = bank[bank_no(l, ("S", g, t))]
                    if p == 2 and t:
                        out = biased[:, g % 2, t - 1, :]
                        dve.tensor_copy(out[:, 2 * P:], b[:, 2 * P:TOK]).then_inc(sems["dve_step"], 1)
                        dve.wait_ge(sems["dve_step"], step(l))
                        dve.tensor_tensor(out[:, 0:2 * P], b[:, 0:2 * P], bias[:, t - 1, h, :], ALU.add) \
                            .then_inc(bank_read[bank_no(l, ("S", g, t))], 1)
                        dve.wait_ge(*once_read(l, ("S", g, t)))
                        dve.tensor_reduce(rowmax[:, t:t + 1], out, AX, ALU.max).then_inc(sems["dve_step"], 1)
                        dve.wait_ge(sems["dve_step"], step(l))
                    else:
                        n = P if t == 0 else TOK
                        dve.tensor_reduce(rowmax[:, t:t + 1], b[:, 0:n], AX, ALU.max).then_inc(sems["dve_step"], 1)
                        dve.wait_ge(sems["dve_step"], step(l))
                scale = -MLA_SCALE if p < 2 else -1.0
                dve.tensor_scalar(negmax[:, g, :], rowmax[:], scale, None, ALU.mult).then_inc(sems["negmax_ready"], 1)
                dve.wait_ge(sems["negmax_ready"], nth(l, "negmax_ready", g + 1))

            def outputs(l, g):
                p, h = GROUPS[g]
                dve.reciprocal(rowsum[:, g, :], rowsum[:, g, :]).then_inc(sems["dve_step"], 1)
                dve.wait_ge(sems["dve_step"], step(l))
                dve.wait_ge(*once_full(l, ("O", g)))
                b = bank[bank_no(l, ("O", g))][:, 0:3 * VD].rearrange("p (t n) -> p t n", t=3)
                col = (4 * p + h) * VD
                dve.tensor_tensor(xn[:, :, col:col + VD], b, last(rowsum[:, g, :], VD), ALU.mult) \
                    .then_inc(bank_read[bank_no(l, ("O", g))], 1)

            def router(l):
                e4 = lambda ap: ap.rearrange("p (a k) -> p a k", k=EPG)
                dve.wait_ge(*once_read(l, ("router",)))
                s = e4(sel[:])
                dve.tensor_tensor(sel[:].rearrange("p (t n) -> p t n", t=TILES), aff[:].rearrange("p (t n) -> p t n", t=TILES),
                                         br[:].unsqueeze(1).broadcast_to([P, TILES, NE]), ALU.add) \
                                             .then_inc(sems["dve_step"], 1)
                dve.wait_ge(sems["dve_step"], step(l))
                n = TILES * NG
                hi, lo = rt[:, 0, 0:2 * n].rearrange("p (a k) -> p a k", k=2), rt[:, 1, 0:2 * n].rearrange("p (a k) -> p a k", k=2)
                dve.tensor_tensor(hi, s[:, :, 0::2], s[:, :, 1::2], ALU.max).then_inc(sems["dve_step"], 1)
                dve.wait_ge(sems["dve_step"], step(l))
                dve.tensor_tensor(lo, s[:, :, 0::2], s[:, :, 1::2], ALU.min).then_inc(sems["dve_step"], 1)
                dve.wait_ge(sems["dve_step"], step(l))
                m1, m2, m3 = (last(rt[:, 2, i * n:(i + 1) * n], 1) for i in range(3))
                dve.tensor_tensor(m1, hi[:, :, 0:1], hi[:, :, 1:2], ALU.max).then_inc(sems["dve_step"], 1)
                dve.wait_ge(sems["dve_step"], step(l))
                dve.tensor_tensor(m2, hi[:, :, 0:1], hi[:, :, 1:2], ALU.min).then_inc(sems["dve_step"], 1)
                dve.wait_ge(sems["dve_step"], step(l))
                dve.tensor_tensor(m3, lo[:, :, 0:1], lo[:, :, 1:2], ALU.max).then_inc(sems["dve_step"], 1)
                dve.wait_ge(sems["dve_step"], step(l))
                dve.tensor_tensor(m2, m2, m3, ALU.max).then_inc(sems["dve_step"], 1)
                dve.wait_ge(sems["dve_step"], step(l))
                score = rt[:, 3, 0:n]
                dve.tensor_tensor(last(score, 1), m1, m2, ALU.add).then_inc(sems["dve_step"], 1)
                dve.wait_ge(sems["dve_step"], step(l))
                s3 = score.rearrange("p (t g) -> p t g", g=NG)
                top = rt[:, 3, n:n + TILES]
                dve.tensor_reduce(top, s3, AX, ALU.max).then_inc(sems["dve_step"], 1)
                dve.wait_ge(sems["dve_step"], step(l))
                dve.tensor_tensor(s3, s3, last(top, NG), ALU.is_equal).then_inc(sems["dve_step"], 1)
                dve.wait_ge(sems["dve_step"], step(l))
                dve.tensor_tensor(s3, s3, tiew[:].unsqueeze(1).broadcast_to([P, TILES, NG]), ALU.mult) \
                    .then_inc(sems["dve_step"], 1)
                dve.wait_ge(sems["dve_step"], step(l))
                dve.tensor_reduce(top, s3, AX, ALU.max).then_inc(sems["dve_step"], 1)
                dve.wait_ge(sems["dve_step"], step(l))
                dve.tensor_tensor(s3, s3, last(top, NG), ALU.is_equal).then_inc(sems["dve_step"], 1)
                dve.wait_ge(sems["dve_step"], step(l))
                rank, cmp = e4(rt[:, 4, :]), e4(rt[:, 5, :])
                dve.memset(rt[:, 4, :], 0.0).then_inc(sems["dve_step"], 1)
                dve.wait_ge(sems["dve_step"], step(l))
                for j in range(EPG):
                    sj = s[:, :, j:j + 1]
                    if j:
                        dve.tensor_tensor(cmp[:, :, 0:j], sj.broadcast_to([P, n, j]), s[:, :, 0:j], ALU.is_gt) \
                            .then_inc(sems["dve_step"], 1)
                        dve.wait_ge(sems["dve_step"], step(l))
                        dve.tensor_tensor(rank[:, :, 0:j], rank[:, :, 0:j], cmp[:, :, 0:j], ALU.add) \
                            .then_inc(sems["dve_step"], 1)
                        dve.wait_ge(sems["dve_step"], step(l))
                    if j < EPG - 1:
                        k = EPG - 1 - j
                        dve.tensor_tensor(cmp[:, :, j + 1:], sj.broadcast_to([P, n, k]), s[:, :, j + 1:], ALU.is_ge) \
                            .then_inc(sems["dve_step"], 1)
                        dve.wait_ge(sems["dve_step"], step(l))
                        dve.tensor_tensor(rank[:, :, j + 1:], rank[:, :, j + 1:], cmp[:, :, j + 1:], ALU.add) \
                            .then_inc(sems["dve_step"], 1)
                        dve.wait_ge(sems["dve_step"], step(l))
                dve.tensor_scalar(rt[:, 4, :], rt[:, 4, :], float(TOP_K), None, ALU.is_lt) \
                    .then_inc(sems["dve_step"], 1)
                dve.wait_ge(sems["dve_step"], step(l))
                dve.tensor_tensor(e4(chosen[:]), rank, last(score, EPG), ALU.mult).then_inc(sems["chosen"], 1)
                dve.wait_ge(sems["chosen"], nth(l, "chosen", 1))
                dve.tensor_tensor(rt[:, 4, :], chosen[:], aff[:], ALU.mult).then_inc(sems["dve_step"], 1)
                dve.wait_ge(sems["dve_step"], step(l))
                w = rt[:, 4, :].rearrange("p (t n) -> p t n", t=TILES)
                dve.tensor_reduce(top, w, AX, ALU.add).then_inc(sems["dve_step"], 1)
                dve.wait_ge(sems["dve_step"], step(l))
                dve.reciprocal(top, top).then_inc(sems["dve_step"], 1)
                dve.wait_ge(sems["dve_step"], step(l))
                dve.tensor_tensor(gates[:], w, last(top, NE), ALU.mult).then_inc(sems["dve_step"], 1)
                dve.wait_ge(sems["dve_step"], step(l))

            def places(l):
                dve.wait_ge(*once_full(l, ("place",)))
                b = bank[bank_no(l, ("place",))]
                dve.tensor_reduce(crowd[:, 0:1], b[:, TILES * NE:(TILES + 1) * NE], AX, ALU.max) \
                    .then_inc(sems["dve_step"], 1)
                dve.wait_ge(sems["dve_step"], step(l))
                dve.scalar_tensor_tensor(place[:], b[:, 0:TILES * NE], 1.0, chosen[:], ALU.add, ALU.mult) \
                    .then_inc(bank_read[bank_no(l, ("place",))], 1)
                dve.wait_ge(*once_read(l, ("place",)))
                dve.tensor_scalar(place[:], place[:], CAP - 1.0, None, ALU.add).then_inc(sems["dve_step"], 1)
                dve.wait_ge(sems["dve_step"], step(l))
                dve.memset(crowd[:, 1:2], 1.0).then_inc(sems["dve_step"], 1)
                dve.wait_ge(sems["dve_step"], step(l))
                for k in range(1, PASSES):
                    dve.scalar_tensor_tensor(crowd[:, 1:2], crowd[:, 0:1], float(k * CAP), crowd[:, 1:2],
                                                    ALU.is_gt, ALU.add).then_inc(sems["dve_step"], 1)
                    dve.wait_ge(sems["dve_step"], step(l))
                for i, (fixed, a_pass) in enumerate(((0, 1), (LEAD, PER_E * NE),
                                                     (16 * S_EXP // RING, 16 * NE))):
                    dve.tensor_scalar(growth[:, i:i + 1], crowd[0:1, 1:2], float(a_pass), float(fixed),
                                             ALU.mult, ALU.add).then_inc(sems["dve_step"], 1)
                    dve.wait_ge(sems["dve_step"], step(l))
                dve.tensor_tensor(tally[:], tally[:], growth[:], ALU.add).then_inc(sems["dve_step"], 1)
                dve.wait_ge(sems["dve_step"], step(l))
                dve.tensor_copy(tally_i[:], tally[:]).then_inc(passes_counted, 1)
                dve.wait_ge(passes_counted, l.n + 2)

            dve.wait_ge(consts_loaded, N_CONST)
            dve.wait_ge(consts_made, 3 + NG)
            dve.wait_ge(cond_exp, 1)
            dve.tensor_scalar(cond_e[:], cond_e[:], 1.0, None, ALU.add).then_inc(cond_exp, 1)
            dve.wait_ge(cond_exp, 2)
            dve.reciprocal(cond_e[:], cond_e[:]).then_inc(cond_exp, 1)
            dve.wait_ge(cond_exp, 3)
            dve.tensor_tensor(condT[:], condT[:], cond_e[:], ALU.mult).then_inc(cond_ready, 1)
            dve.memset(tally[:], 0.0).then_inc(consts_made, 1)
            dve.wait_ge(consts_made, 4 + NG)
            dve.tensor_copy(tally_i[:], tally[:]).then_inc(passes_counted, 1)
            dve.wait_ge(passes_counted, 1)
            for i in range(SPLIT):
                dve.sem_inc(hi_made[i], 2)
                dve.sem_inc(lo_made[i], 2)
                dve.sem_inc(split_used[i], 1)
            with dve.Fori(0, DEPTH) as n:
                count[0] = 0
                dve.wait_ge(passes_counted, n + 1)
                dve.sem_inc(carried, 1)
                l = layer_at(dve, n)
                normalise(l, "norm1", 1)
                dve.wait_ge(sems["small_loaded"], nth(l, "small_loaded", PER_LAYER["small_loaded"]))
                for m in range(6):
                    dve.wait_ge(*once_full(l, ("mod", m)))
                    b = bank[bank_no(l, ("mod", m))]
                    ada_b = vecs[:, V_ADA + m * KC:V_ADA + (m + 1) * KC]
                    dve.tensor_tensor(modT[:, m, :, :], b[:, 0:2 * KC].rearrange("p (c q) -> p c q", q=2),
                                            last(ada_b, 2), ALU.add).then_inc(bank_read[bank_no(l, ("mod", m))], 1)
                    dve.wait_ge(*once_read(l, ("mod", m)))
                for k, (a, at, m) in enumerate(((a1, V_N1, 1), (a2, V_N2, 4))):
                    dve.scalar_tensor_tensor(a[:], modT[:, m, :, :], 1.0, last(vecs[:, at:at + KC], 2),
                                                     ALU.add, ALU.mult).then_inc(sems["mod_ready"], 1)
                    dve.wait_ge(sems["mod_ready"], nth(l, "mod_ready", k + 1))
                modulate(l, "n1", a1, 0)
                dve.wait_ge(sems["bias_loaded"], nth(l, "bias_loaded", PER_LAYER["bias_loaded"]))
                bias_rows = bias[:, :, :, :].rearrange("p t h (j k) -> p (t h j) k", k=GRID_W)
                dve.tensor_tensor(bias_rows, bias_rows, mask[:].unsqueeze(1).broadcast_to([P, 32, GRID_W]), ALU.add) \
                    .then_inc(sems["dve_step"], 1)
                dve.wait_ge(sems["dve_step"], step(l))
                for q, (at, n) in enumerate(((0, QL), (O_KV, KVL))):
                    for t in range(TILES):
                        dve.wait_ge(*once_read(l, ("proj", q, t)))
                        src = proj[:, t, at:at + n]
                        dve.tensor_tensor_reduce(squares[:, 0:n], src, src, 1.0, 0.0, ALU.mult, ALU.add,
                                                        ssum[:, 3 * q + t:3 * q + t + 1]) \
                                                            .then_inc(sems["dve_step"], 1)
                        dve.wait_ge(sems["dve_step"], step(l))
                dve.tensor_scalar(ssum[:, 3:6], ssum[:, 3:6], QL / KVL, None, ALU.mult).then_inc(sems["dve_step"], 1)
                dve.wait_ge(sems["dve_step"], step(l))
                mean_squares(l, "latent", 6, QL)
                dve.wait_ge(sems["rstd_ready"], nth(l, "rstd_ready", RMS.index("latent") + 1))
                for t in range(TILES):
                    dve.tensor_scalar(q_lat_n[:, t, :], proj[:, t, 0:QL], rstd[:, t:t + 1], None, ALU.mult) \
                        .then_inc(sems["dve_step"], 1)
                    dve.wait_ge(sems["dve_step"], step(l))
                for t in range(TILES):
                    ins = dve.scalar_tensor_tensor(ckvn[:, t, :], proj[:, t, O_KV:O_KV + KVL], rstd[:, 3 + t:4 + t],
                                                   rowv[:, R_KV:R_KV + KVL], ALU.mult, ALU.mult)
                ins.then_inc(sems["latents_normed"], 1)
                dve.wait_ge(sems["latents_normed"], nth(l, "latents_normed", 1))
                for c in range(2):
                    dve.wait_ge(*once_full(l, ("ql", c)))
                    b = bank[bank_no(l, ("ql", c))]
                    dve.tensor_scalar(qlatT[:, c, :], b[:, 0:TOK], vecs[:, V_QAG + c:V_QAG + c + 1], None, ALU.mult) \
                        .then_inc(bank_read[bank_no(l, ("ql", c))], 1)
                dve.wait_ge(*once_full(l, ("ckv",)))
                b = bank[bank_no(l, ("ckv",))]
                dve.tensor_copy(ckvT[:, 0:TOK], b[:, 0:TOK]).then_inc(bank_read[bank_no(l, ("ckv",))], 1)
                dve.wait_ge(sems["gate_sigmoid"], nth(l, "gate_sigmoid", 1))
                dve.tensor_tensor(glu, proj[:, :, O_A:O_A + CONV_CH], proj[:, :, O_G:O_G + CONV_CH], ALU.mult) \
                    .then_inc(sems["glu_ready"], 1)
                dve.wait_ge(sems["glu_ready"], nth(l, "glu_ready", 1))
                for c in range(2):
                    dve.wait_ge(*once_full(l, ("conv", c)))
                    b = bank[bank_no(l, ("conv", c))]
                    dve.tensor_copy(conv_in[:, c, C_CTX:C_CTX + P], b[:, 0:P]).then_inc(sems["dve_step"], 1)
                    dve.wait_ge(sems["dve_step"], step(l))
                    dve.tensor_copy(conv_in[:, c, C_LAT:C_LAT + 2 * P], b[:, P:TOK]) \
                        .then_inc(bank_read[bank_no(l, ("conv", c))], 1)
                head_sums(l, 0)
                head_gains(l, 0)
                head_scales(l, 0)
                for i in range(len(GROUPS) + 2):
                    if i < len(GROUPS):
                        maxima(l, i)
                    for k in range(max(6 * (i - 2), 0), max(min(6 * (i - 1), TAPS), 0)):
                        tap = vecs[:, V_TAP + 2 * k:V_TAP + 2 * k + 1]
                        if k == 0:
                            dve.tensor_scalar(conv_acc[:, 0, :], conv_in[:, 0, 0:C_OUT], tap,
                                                     vecs[:, V_DWB:V_DWB + 1], ALU.mult, ALU.add) \
                                                         .then_inc(sems["dve_step"], 1)
                            dve.wait_ge(sems["dve_step"], step(l))
                        else:
                            ins = dve.scalar_tensor_tensor(conv_acc[:, 0, :], conv_in[:, 0, k:k + C_OUT], tap,
                                                           conv_acc[:, 0, :], ALU.mult, ALU.add)
                            if k < TAPS - 1:
                                ins.then_inc(sems["dve_step"], 1)
                                dve.wait_ge(sems["dve_step"], step(l))
                            else:
                                ins.then_inc(sems["conv_lower"], 1)
                                dve.wait_ge(sems["conv_lower"], nth(l, "conv_lower", 1))
                    if i == 7:
                        dve.wait_ge(sems["conv_steps"], nth(l, "conv_steps", 2 * TAPS))
                    if i in (0, 5):
                        head_sums(l, 1 + i // 5)
                    if i in (1, 5):
                        head_gains(l, 1 + i // 5)
                    if i in (2, 6):
                        head_scales(l, 1 + i // 5)
                    if 1 <= i <= len(GROUPS):
                        dve.wait_ge(*once_full(l, ("PT", i - 1, 0)))
                        b = bank[bank_no(l, ("PT", i - 1, 0))]
                        dve.tensor_copy(probsT[:, (i - 1) % 2, 0:4 * P], b[:, :]) \
                            .then_inc(bank_read[bank_no(l, ("PT", i - 1, 0))], 1)
                    if i >= 2:
                        outputs(l, i - 2)
                    if i == 9:
                        for t in range(TILES):
                            dve.wait_ge(*once_full(l, ("cb", t)))
                            b = bank[bank_no(l, ("cb", t))]
                            dve.bn_stats(stats[:, t, :], b[:, 0:CONV_CH]).then_inc(sems["dve_step"], 1)
                            dve.wait_ge(sems["dve_step"], step(l))
                            dve.sem_inc(carried, 1)
                            dve.bn_aggr(meanvar[:, t, :], stats[:, t, :]).then_inc(sems["dve_step"], 1)
                            dve.wait_ge(sems["dve_step"], step(l))
                        dve.tensor_copy(ssum[:, 0:TILES], meanvar[:, :, 1]).then_inc(sems["dve_step"], 1)
                        dve.wait_ge(sems["dve_step"], step(l))
                        mean_squares(l, "conv", TILES, 1)
                        dve.wait_ge(sems["rstd_ready"], nth(l, "rstd_ready", RMS.index("conv") + 1))
                        for t in range(TILES):
                            dve.wait_ge(*once_full(l, ("cb", t)))
                            b = bank[bank_no(l, ("cb", t))]
                            dve.tensor_scalar(ln_tm[:, t, :], b[:, 0:CONV_CH], meanvar[:, t, 0:1], rstd[:, t:t + 1],
                                                    ALU.subtract, ALU.mult) \
                                                        .then_inc(bank_read[bank_no(l, ("cb", t))], 1)
                    if i == 10:
                        for c in range(2):
                            dve.wait_ge(*once_full(l, ("ln", c)))
                            b = bank[bank_no(l, ("ln", c))]
                            dve.tensor_scalar(z_conv[:, c, :], b[:, 0:TOK], vecs[:, V_LNG + c:V_LNG + c + 1],
                                                    vecs[:, V_LNB + c:V_LNB + c + 1], ALU.mult, ALU.add) \
                                                        .then_inc(bank_read[bank_no(l, ("ln", c))], 1)
                            dve.wait_ge(*once_read(l, ("ln", c)))
                dve.wait_ge(*once_read(l, ("g1", 1, 1)))
                for j in range(OUT_SLOTS):
                    for t in range(TILES):
                        dve.wait_ge(*once_full(l, ("out", j, t)))
                        b = bank[bank_no(l, ("out", j, t))]
                        cols = slice(j * 256, (j + 1) * 256)
                        dve.tensor_tensor(scratch[:, 0:256], b[:, 0:256], G[:, min(t, 1), cols], ALU.mult) \
                            .then_inc(bank_read[bank_no(l, ("out", j, t))], 1)
                        dve.wait_ge(*once_read(l, ("out", j, t)))
                        ins = dve.tensor_tensor(x[:, t, cols], x[:, t, cols], scratch[:, 0:256], ALU.add)
                        if j == OUT_SLOTS - 1:
                            ins.then_inc(sems["x_mid"], 1)
                            dve.wait_ge(sems["x_mid"], nth(l, "x_mid", t + 1))
                        else:
                            ins.then_inc(sems["dve_step"], 1)
                            dve.wait_ge(sems["dve_step"], step(l))
                normalise(l, "norm2", 2)
                modulate(l, "n2", a2, 3)
                router(l)
                for t in range(TILES):
                    for q in range(2):
                        dve.wait_ge(*once_full(l, ("h", t, q)))
                        b = bank[bank_no(l, ("h", t, q))]
                        dve.wait_ge(sems["h_hi_made"], nth(l, "h_hi_made", 2 * t + q + 1))
                        cols = slice(q * 512, (q + 1) * 512)
                        dve.tensor_tensor(h_lo[:, t, cols], b[:, :], h_hi[:, t, cols], ALU.subtract) \
                            .then_inc(bank_read[bank_no(l, ("h", t, q))], 1)
                places(l)
                dve.wait_ge(sems["acc_cleared"], nth(l, "acc_cleared", 1))

                def split_rest(v, i):
                    dve.wait_ge(*once_hi(v, i))
                    dve.wait_ge(*once_split_free(v, i))
                    dve.tensor_tensor(w_lo[:, split_no(v, i), :], ring[:, i, :], w_hi[:, split_no(v, i), :],
                                      ALU.subtract).then_inc(lo_made[split_no(v, i)], 1)

                def pick_tokens(v, first=False):
                    if not first:
                        dve.wait_ge(*once_full(before(v), ("ST",)))
                    at = place[:, :].rearrange("p (t n) -> p t n", t=TILES)
                    at = at[:, :, v.k:v.k + 1] if v.pair is None else at[:, :, bass.ds(v.pair * 2 + v.k, 1)]
                    dve.tensor_tensor(pick[:], shapes[:, 1:2, :].broadcast_to([P, TILES, P]),
                                      at.broadcast_to([P, TILES, P]), ALU.is_equal).then_inc(pick_made, 1)

                def gathered_rest(v):
                    for k in (1, 3):
                        dve.wait_ge(*once_full(v, ("gather", k)))
                        b = bank[bank_no(v, ("gather", k))]
                        dve.tensor_copy(hg_lo[:, 2 * k - 2:2 * k + 2, :].rearrange("p c n -> p (c n)"), b[:, :]) \
                            .then_inc(bank_read[bank_no(v, ("gather", k))], 1)

                def hidden(v):
                    dve.wait_ge(*once_full(v, ("U",)))
                    b = bank[bank_no(v, ("U",))]
                    dve.wait_ge(*once_read(v, ("G",)))
                    dve.tensor_tensor(sg[:], b[:, :], sg[:], ALU.mult).then_inc(bank_read[bank_no(v, ("U",))], 1)

                def accumulate(v, turns):
                    g = gates[:, :, v.k:v.k + 1] if v.pair is None else gates[:, :, bass.ds(v.pair * 2 + v.k, 1)]
                    for k in turns:
                        t, n = k // 2, k % 2
                        dve.wait_ge(*once_full(v, ("scatter", k)))
                        b = bank[bank_no(v, ("scatter", k))]
                        part = acc[:, t, n * 512:(n + 1) * 512]
                        dve.scalar_tensor_tensor(part, b[:, :], g[:, t, :], part, ALU.mult, ALU.add) \
                            .then_inc(bank_read[bank_no(v, ("scatter", k))], 1)

                def finish_expert(v, follows=True):
                    if v.pair is not None or v.k > 0:
                        accumulate(before(v), range(SCAT // 2))
                    dve.wait_ge(*once_full(v, ("T",)))
                    b = bank[bank_no(v, ("T",))]
                    dve.wait_ge(hidT_hi_made, visits(v, 1, 1))
                    dve.tensor_tensor(hidT_lo[:, :, :].rearrange("p c n -> p (c n)"), b[:, :],
                                            hidT_hi[:, :, :].rearrange("p c n -> p (c n)"), ALU.subtract) \
                                                .then_inc(bank_read[bank_no(v, ("T",))], 1)
                    if v.pair is not None or v.k > 0:
                        accumulate(before(v), range(SCAT // 2, SCAT))
                    if follows:
                        pick_tokens(after(v))
                        split_rest(after(v), 0)
                    for n in range(2):
                        dve.wait_ge(*once_full(v, ("Y", n)))
                        b = bank[bank_no(v, ("Y", n))]
                        dve.wait_ge(y_hi_made, visits(v, 2, n + 1))
                        cols = slice(n * 512, (n + 1) * 512)
                        dve.tensor_tensor(y_lo[:, cols], b[:, :], y_hi[:, cols], ALU.subtract) \
                            .then_inc(bank_read[bank_no(v, ("Y", n))], 1)
                    if follows:
                        gathered_rest(after(v))
                        split_rest(after(v), 2)
                        split_rest(after(v), 3)
                        split_rest(after(v), 5)
                        hidden(after(v))

                dve.sem_inc(carried, 1)
                end = dve.value_load(tally_i[0:1, 0:1], min_val=0, max_val=DEPTH * PASSES)
                with dve.Fori(l.passes, end) as w:
                    dve.tensor_scalar(place[:], place[:], -float(CAP), None, ALU.add).then_inc(placed, 1)
                    dve.wait_ge(placed, w + 1)
                    v = Visit(l, w, None, 0)
                    pick_tokens(v, first=True)
                    split_rest(v, 0)
                    gathered_rest(v)
                    split_rest(v, 2)
                    split_rest(v, 3)
                    split_rest(v, 5)
                    hidden(v)
                    finish_expert(v)
                    with dve.Fori(0, NE // 2 - 1) as pair:
                        for k in range(1, 3):
                            finish_expert(Visit(l, w, pair, k))
                    v = Visit(l, w, None, NE - 1)
                    finish_expert(v, follows=False)
                    accumulate(v, range(SCAT))
                    dve.wait_ge(*once_read(v, ("scatter", SCAT - 1)))
                dve.wait_ge(*once_read(l, ("g2", 1, 1)))
                for t in range(TILES):
                    dve.tensor_tensor(acc[:, t, :], acc[:, t, :], G[:, min(t, 1), :], ALU.mult) \
                        .then_inc(sems["dve_step"], 1)
                    dve.wait_ge(sems["dve_step"], step(l))
                    ins = dve.tensor_tensor(x[:, t, :], x[:, t, :], acc[:, t, :], ALU.add)
                    if t < TILES - 1:
                        ins.then_inc(sems["dve_step"], 1)
                        dve.wait_ge(sems["dve_step"], step(l))
                ins.then_inc(sems["x_done"], 1)
            assert count[0] == DVE_STEPS, count[0]


def _layout(i):
    f = {k: np.ascontiguousarray(v) for k, v in i.items()}
    L = DEPTH
    wring = np.zeros((L, LAYER_SLOTS, P, SLOT), np.float32)

    def by_columns(w, n):
        return w.reshape(L, KC, P, -1, n).transpose(0, 3, 2, 1, 4).reshape(L, -1, P, KC * n)

    wring[:, 0:S_IN] = by_columns(f["w_ada"], 256)
    full = 256 * (IN_SLOTS - 1)
    wring[:, S_IN:S_UP - 1] = by_columns(f["w_in"][:, :, :full], 256)
    wring[:, S_UP - 1, :, :KC * LAST_W] = by_columns(f["w_in"][:, :, full:], LAST_W)[:, 0]
    wring[:, S_UP - 1, :, KC * LAST_W:KC * LAST_W + 512] = f["w_kv_up"][:, :, 512:]
    wring[:, S_UP, :, :1536] = f["w_q_up"].reshape(L, 2, P, 768).transpose(0, 2, 1, 3).reshape(L, P, 1536)
    wring[:, S_UP, :, 1536:] = f["w_kv_up"][:, :, :512]
    wring[:, S_OUT:S_EXP] = by_columns(f["w_out"], 256)
    ex = wring[:, S_EXP:].reshape(L, NE, PER_EXPERT, P, SLOT)
    for s, name, k in ((0, "w_e_gate", 4), (2, "w_e_up", 4), (4, "w_e_down", 2)):
        w = f[name]
        ex[:, :, s:s + 2] = w.reshape(L, NE, 2, k, P, -1).transpose(0, 1, 2, 4, 3, 5).reshape(L, NE, 2, P, SLOT)

    def columns(v):
        return v.reshape(L, -1, P).transpose(0, 2, 1)

    vec = np.concatenate([columns(f[n]) for n in ("b_ada", "norm1_g", "norm2_g", "conv_dw_b", "conv_ln_g",
                                                  "conv_ln_b", "q_a_g")] + [columns(f["conv_dw_w"].reshape(L, -1))], 2)
    rows = np.concatenate([f[n] for n in ("mla_q_norm_g", "mla_k_norm_g", "na_q_norm_g", "na_k_norm_g", "kv_a_g")], 1)
    rpb = f["na_rpb"]
    far = GRID_W - WIN_W
    padded = np.pad(rpb, ((0, 0), (0, 0), (0, 0), (far, far)))
    at = GRID_W - 1 + np.arange(GRID_W)[None, :] - np.arange(GRID_W)[:, None]
    na_bias = padded[:, :, :, at].transpose(0, 3, 1, 2, 4)
    tok = np.arange(2 * P)
    inv = (10000.0 ** (-np.arange(ROPE // 4, dtype=np.float32) / (ROPE // 4))).astype(np.float32)
    ang = np.concatenate([(tok // GRID_W).astype(np.float32)[:, None] * inv,
                          (tok % GRID_W).astype(np.float32)[:, None] * inv], 1)
    cos, sin = np.cos(ang), np.sin(ang)
    table = np.stack([np.repeat(cos, 2, 1), np.stack([-sin, sin], 2).reshape(2 * P, ROPE)], 1)
    rope = table.reshape(2, P, 2, ROPE).transpose(1, 0, 2, 3)
    places = np.where(np.arange(P) < CAP, np.arange(P), -1000)
    shape_consts = np.stack([np.eye(P), np.tile(places, (P, 1)), np.triu(np.ones((P, P)), 1)], 1)
    q = np.arange(P) % GRID_W
    c0 = np.clip(q - WIN_W // 2, 0, GRID_W - WIN_W)
    k = np.arange(GRID_W)
    mask = np.where((k[None] >= c0[:, None]) & (k[None] < c0[:, None] + WIN_W), 0.0, MASKED)
    x = np.concatenate([f["x_prompt"][0], f["x_sample"][0]], 0).reshape(TILES, P, D_MODEL).transpose(1, 0, 2)
    cond = np.stack([f["c_ctx"].reshape(KC, P).T, f["c"][0].reshape(KC, P).T], 2)
    out = dict(
        wring=wring.reshape(L * LAYER_SLOTS, P, SLOT), x_in=x, vec=vec, rows=rows,
        ckv_cache=f["cache_mla_ckv"][0].transpose(0, 2, 1), kr_cache=f["cache_mla_krope"][0],
        nak_cache=f["cache_na_k"][0].transpose(0, 3, 2, 1), nav_cache=f["cache_na_v"][0], cond=cond,
        w_router=f["w_router"].reshape(KC, P, NE).transpose(1, 0, 2), b_router=f["b_router"],
        rope=rope, shape_consts=shape_consts, na_mask=mask, na_bias=na_bias)
    return {n: np.ascontiguousarray(a, dtype=np.float32) for n, a in out.items()}


OUTS = dict(y_prompt=(P, D_MODEL), y_sample=(2 * P, D_MODEL), new_ckv=(DEPTH, P, KVL), new_krope=(DEPTH, P, ROPE),
            new_nak=(DEPTH, P, NAH * NAD), new_nav=(DEPTH, P, NAH * NAD))


def program(nc, arrays):
    args = {n: nc.dram_tensor(n + "_dram", a.shape, F32, kind="ExternalInput").ap() for n, a in arrays.items()}
    outs = {n: nc.dram_tensor(n + "_dram", s, F32, kind="ExternalOutput").ap() for n, s in OUTS.items()}
    build(nc, **args, **outs)


def kernel(**inputs):
    import concourse.bacc as bacc
    from concourse.bass_utils import run_bass_kernel_spmd

    nc = bacc.Bacc("TRN2", target_bir_lowering=False, num_devices=1)
    arrays = _layout({k: np.asarray(v) for k, v in inputs.items()})
    program(nc, arrays)
    r = run_bass_kernel_spmd(nc, [{n + "_dram": a for n, a in arrays.items()}], core_ids=[0])
    got = {n: r.results[0][n + "_dram"] for n in OUTS}
    return (got["y_prompt"].reshape(1, P, D_MODEL), got["y_sample"].reshape(1, 2 * P, D_MODEL),
            got["new_ckv"].reshape(1, DEPTH, P, KVL), got["new_krope"].reshape(1, DEPTH, P, ROPE),
            got["new_nak"].reshape(1, DEPTH, P, NAH, NAD), got["new_nav"].reshape(1, DEPTH, P, NAH, NAD))
```
